# Optimizing a Trainium2 kernel written in Bass

```python
import jax
import jax.numpy as jnp
from jax import lax

D_MODEL = 1024
BATCH = 1
SEQ = 1024
DEPTH = 1

GRID_W = 64
CTX_LEN = 256
CHUNK = 128
GMLP_HEADS = 4
GMLP_W = D_MODEL // 2
GMLP_DH = GMLP_W // GMLP_HEADS
MLSTM_HEADS = 4
MLSTM_W = D_MODEL // 2
MLSTM_DH = MLSTM_W // MLSTM_HEADS
D_MIX = GMLP_W + MLSTM_W
CONV_W = 3
N_EXPERTS = 16
EC_FACTOR = 2
D_EXPERT = 2 * D_MODEL
EPS = 1e-6

U_COL = 0
VG_COL = GMLP_W
Q_COL = 2 * GMLP_W
O_COL = Q_COL + MLSTM_W
K_COL = O_COL + MLSTM_W
PROJ_W = K_COL + 2 * MLSTM_W + 4 * MLSTM_HEADS

kernel_name = 'hybrid_gmlp_mlstm_expert_choice_dit_block'

def rms_norm(x, g):
    xf = x.astype(jnp.float32)
    y = xf * lax.rsqrt(jnp.mean(xf * xf, axis=-1, keepdims=True) + EPS)
    return (y * g).astype(x.dtype)

def layer_norm_plain(x):
    xf = x.astype(jnp.float32)
    mu = jnp.mean(xf, axis=-1, keepdims=True)
    var = jnp.mean(jnp.square(xf - mu), axis=-1, keepdims=True)
    return ((xf - mu) * lax.rsqrt(var + EPS)).astype(x.dtype)

def adaln(cond, w, b, n):
    m = jax.nn.silu(cond) @ w[:, :n * D_MODEL] + b[:n * D_MODEL]
    return jnp.split(m, n, axis=-1)

def centred_dwconv(x, w):
    k = w.shape[0]
    pad = k // 2
    n = x.shape[1]
    xp = jnp.pad(x, ((0, 0), (pad, pad), (0, 0)))
    return sum(xp[:, j:j + n] * w[j] for j in range(k))

def to_heads(a, n_heads):
    b, n, w = a.shape
    return a.reshape(b, n, n_heads, w // n_heads).transpose(0, 2, 1, 3)

def gmlp_mix(u_pre, v_pre, ws, bs, n_chunks):
    b, n, _ = u_pre.shape
    u = jax.nn.gelu(u_pre)
    v = layer_norm_plain(jax.nn.gelu(v_pre))
    v = v.reshape(b, n_chunks, CHUNK, GMLP_HEADS, GMLP_DH)
    s = jnp.einsum('hpq,bnqhd->bnphd', ws, v) + bs.T[None, None, :, :, None]
    return u * s.reshape(b, n, GMLP_W)

def zero_state(b):
    return (jnp.zeros((b, MLSTM_HEADS, MLSTM_DH, MLSTM_DH), jnp.float32),
            jnp.zeros((b, MLSTM_HEADS, MLSTM_DH), jnp.float32),
            jnp.zeros((b, MLSTM_HEADS), jnp.float32))

def mlstm_kv_gates(p_kv, conv_k, b_i, b_f):
    b, n, _ = p_kv.shape
    k = jax.nn.silu(centred_dwconv(p_kv[..., :MLSTM_W], conv_k)) * (MLSTM_DH ** -0.5)
    v = p_kv[..., MLSTM_W:2 * MLSTM_W]
    g0 = 2 * MLSTM_W
    i_pre = p_kv[..., g0:g0 + 2 * MLSTM_HEADS].astype(jnp.float32).reshape(b, n, 2, MLSTM_HEADS) + b_i
    f_pre = p_kv[..., g0 + 2 * MLSTM_HEADS:].astype(jnp.float32).reshape(b, n, 2, MLSTM_HEADS) + b_f
    log_i = jnp.transpose(i_pre, (2, 0, 3, 1))
    log_f = jax.nn.log_sigmoid(jnp.transpose(f_pre, (2, 0, 3, 1)))
    return to_heads(k, MLSTM_HEADS), to_heads(v, MLSTM_HEADS), log_i, log_f

def mlstm_scan(q, k, v, log_i, log_f, state):
    b, h, n, dh = q.shape
    nc = n // CHUNK

    def to_chunks(a):
        a = a.astype(jnp.float32)
        return jnp.moveaxis(a.reshape((b, h, nc, CHUNK) + a.shape[3:]), 2, 0)

    xs = tuple(to_chunks(a) for a in (q, k, v, log_i, log_f))
    causal = jnp.tril(jnp.ones((CHUNK, CHUNK), dtype=bool))

    def step(carry, inp):
        c_prev, n_prev, m_prev = carry
        qc, kc, vc, li, lf = inp
        bcum = jnp.cumsum(lf, axis=-1)
        g = bcum + m_prev[..., None]
        dmat = jnp.where(causal, bcum[..., :, None] - bcum[..., None, :] + li[..., None, :], -jnp.inf)
        m_t = jnp.maximum(g, jnp.max(dmat, axis=-1))
        inter = jnp.exp(g - m_t)
        s = jnp.einsum('bhtd,bhsd->bhts', qc, kc) * jnp.exp(dmat - m_t[..., None])
        num = inter[..., None] * jnp.einsum('bhvd,bhtd->bhtv', c_prev, qc) + jnp.einsum('bhts,bhsv->bhtv', s, vc)
        den = inter * jnp.einsum('bhd,bhtd->bht', n_prev, qc) + jnp.sum(s, axis=-1)
        h_out = num / jnp.maximum(jnp.abs(den), jnp.exp(-m_t))[..., None]
        b_last = bcum[..., -1]
        a = b_last[..., None] - bcum + li
        m_new = jnp.maximum(b_last + m_prev, jnp.max(a, axis=-1))
        decay = jnp.exp(b_last + m_prev - m_new)
        wk = jnp.exp(a - m_new[..., None])[..., None] * kc
        c_new = decay[..., None, None] * c_prev + jnp.einsum('bhsv,bhsd->bhvd', vc, wk)
        n_new = decay[..., None] * n_prev + jnp.sum(wk, axis=2)
        return (c_new, n_new, m_new), h_out

    state, hs = lax.scan(step, state, xs)
    return jnp.moveaxis(hs, 0, 2).reshape(b, h, n, dh), state

def mlstm_state_from_zero(k, v, log_i, log_f):
    k = k.astype(jnp.float32)
    v = v.astype(jnp.float32)
    bcum = jnp.cumsum(log_f, axis=-1)
    b_last = bcum[..., -1]
    a = b_last[..., None] - bcum + log_i
    m = jnp.maximum(b_last, jnp.max(a, axis=-1))
    wk = jnp.exp(a - m[..., None])[..., None] * k
    return (jnp.einsum('bhsv,bhsd->bhvd', v, wk), jnp.sum(wk, axis=2), m)

def head_norm(h, g):
    mu = jnp.mean(h, axis=-1, keepdims=True)
    var = jnp.mean(jnp.square(h - mu), axis=-1, keepdims=True)
    hn = (h - mu) * lax.rsqrt(var + EPS)
    b, nh, n, dh = h.shape
    return hn.transpose(0, 2, 1, 3).reshape(b, n, nh * dh) * g

def hybrid_mixer(p, n_chunks, conv_q, conv_k, b_i, b_f, ws, bs, norm_g, w_out, st_f, st_b):
    y_g = gmlp_mix(p[..., U_COL:U_COL + GMLP_W], p[..., VG_COL:VG_COL + GMLP_W], ws, bs, n_chunks)
    q = to_heads(jax.nn.silu(centred_dwconv(p[..., Q_COL:Q_COL + MLSTM_W], conv_q)), MLSTM_HEADS)
    o = jax.nn.sigmoid(p[..., O_COL:O_COL + MLSTM_W])
    k, v, log_i, log_f = mlstm_kv_gates(p[..., K_COL:], conv_k, b_i, b_f)
    h_f, st_f = mlstm_scan(q, k, v, log_i[0], log_f[0], st_f)
    h_b, st_b = mlstm_scan(jnp.flip(q, 2), jnp.flip(k, 2), jnp.flip(v, 2),
                           jnp.flip(log_i[1], 2), jnp.flip(log_f[1], 2), st_b)
    h = head_norm(h_f + jnp.flip(h_b, 2), norm_g).astype(p.dtype)
    y_m = o * h
    y = jnp.concatenate([y_g, y_m], axis=-1) @ w_out
    return y, st_f, st_b

def expert_choice_ffn(h, w_router, w_gate, w_up, w_down, capacity):
    n_tok, d = h.shape[1], h.shape[2]
    aff = jax.nn.softmax(jnp.einsum('bnd,de->bne', h, w_router).astype(jnp.float32), axis=-1)
    gate, idx = lax.top_k(jnp.swapaxes(aff, 1, 2), capacity)
    xe = jax.vmap(lambda hb, ib: hb[ib])(h, idx)
    a = jnp.einsum('becd,edf->becf', xe, w_gate)
    u = jnp.einsum('becd,edf->becf', xe, w_up)
    ye = jnp.einsum('becf,efd->becd', jax.nn.silu(a) * u, w_down) * gate[..., None].astype(h.dtype)
    scatter = lambda ib, yb: jnp.zeros((n_tok, d), yb.dtype).at[ib.reshape(-1)].add(yb.reshape(-1, d))
    return jax.vmap(scatter)(idx, ye)

def setup_inputs(seed: int = 0) -> dict:
    key = jax.random.key(seed)
    ks = jax.random.split(key, 22)
    nrm = lambda k, shape, s: jax.random.normal(k, shape, jnp.float32) * s
    f_bias = jnp.linspace(3.0, 6.0, MLSTM_HEADS, dtype=jnp.float32)
    return {
        'x': nrm(ks[0], (BATCH, SEQ, D_MODEL), 1.0),
        'c': nrm(ks[1], (BATCH, D_MODEL), 1.0),
        'ctx': nrm(ks[2], (BATCH, CTX_LEN, D_MODEL), 1.0),
        'c_ctx': nrm(ks[3], (D_MODEL,), 1.0),
        'w_mod': nrm(ks[4], (DEPTH, D_MODEL, 6 * D_MODEL), 0.5 * D_MODEL ** -0.5),
        'b_mod': nrm(ks[5], (DEPTH, 6 * D_MODEL), 0.02),
        'norm_mix_g': 1.0 + nrm(ks[6], (DEPTH, D_MODEL), 0.02),
        'w_in': nrm(ks[7], (DEPTH, D_MODEL, PROJ_W), D_MODEL ** -0.5),
        'conv_q': nrm(ks[8], (DEPTH, CONV_W, MLSTM_W), CONV_W ** -0.5),
        'conv_k': nrm(ks[9], (DEPTH, CONV_W, MLSTM_W), CONV_W ** -0.5),
        'b_igate': nrm(ks[10], (DEPTH, 2, MLSTM_HEADS), 0.1),
        'b_fgate': f_bias + nrm(ks[11], (DEPTH, 2, MLSTM_HEADS), 0.1),
        'gmlp_ws': nrm(ks[12], (DEPTH, GMLP_HEADS, CHUNK, CHUNK), CHUNK ** -0.5),
        'gmlp_bs': 1.0 + nrm(ks[13], (DEPTH, GMLP_HEADS, CHUNK), 0.02),
        'mlstm_norm_g': 1.0 + nrm(ks[14], (DEPTH, MLSTM_W), 0.02),
        'w_out': nrm(ks[15], (DEPTH, D_MIX, D_MODEL), D_MIX ** -0.5),
        'norm_ffn_g': 1.0 + nrm(ks[16], (DEPTH, D_MODEL), 0.02),
        'w_router': nrm(ks[17], (DEPTH, D_MODEL, N_EXPERTS), D_MODEL ** -0.5),
        'w_gate_e': nrm(ks[18], (DEPTH, N_EXPERTS, D_MODEL, D_EXPERT), D_MODEL ** -0.5),
        'w_up_e': nrm(ks[19], (DEPTH, N_EXPERTS, D_MODEL, D_EXPERT), D_MODEL ** -0.5),
        'w_down_e': nrm(ks[20], (DEPTH, N_EXPERTS, D_EXPERT, D_MODEL), D_EXPERT ** -0.5),
        'final_g': 1.0 + nrm(ks[21], (D_MODEL,), 0.02),
    }

def reference(x, c, ctx, c_ctx, w_mod, b_mod, norm_mix_g, w_in, conv_q, conv_k, b_igate, b_fgate,
              gmlp_ws, gmlp_bs, mlstm_norm_g, w_out, norm_ffn_g, w_router, w_gate_e, w_up_e,
              w_down_e, final_g):
    rows = x.shape[1] // GRID_W
    n_lat = rows * GRID_W
    lat_chunks = n_lat // CHUNK
    cap_lat = EC_FACTOR * n_lat // N_EXPERTS
    cap_ctx = EC_FACTOR * ctx.shape[1] // N_EXPERTS
    for l in range(DEPTH):
        h_c = rms_norm(ctx, norm_mix_g[l])
        if l == DEPTH - 1:
            sh_c, sc_c = adaln(c_ctx, w_mod[l], b_mod[l], 2)
            p_c = (h_c * (1.0 + sc_c) + sh_c) @ w_in[l][:, K_COL:]
            k_c, v_c, li_c, lf_c = mlstm_kv_gates(p_c, conv_k[l], b_igate[l], b_fgate[l])
            st_f = mlstm_state_from_zero(k_c, v_c, li_c[0], lf_c[0])
            st_b = mlstm_state_from_zero(jnp.flip(k_c, 2), jnp.flip(v_c, 2),
                                         jnp.flip(li_c[1], 2), jnp.flip(lf_c[1], 2))
        else:
            sh_c, sc_c, g_c, sh2_c, sc2_c, g2_c = adaln(c_ctx, w_mod[l], b_mod[l], 6)
            zero = zero_state(ctx.shape[0])
            y_c, st_f, st_b = hybrid_mixer((h_c * (1.0 + sc_c) + sh_c) @ w_in[l], ctx.shape[1] // CHUNK,
                                           conv_q[l], conv_k[l], b_igate[l], b_fgate[l], gmlp_ws[l],
                                           gmlp_bs[l], mlstm_norm_g[l], w_out[l], zero, zero)
            ctx = ctx + g_c * y_c
            h2_c = rms_norm(ctx, norm_ffn_g[l]) * (1.0 + sc2_c) + sh2_c
            ctx = ctx + g2_c * expert_choice_ffn(h2_c, w_router[l], w_gate_e[l], w_up_e[l], w_down_e[l], cap_ctx)
        sh, sc, g, sh2, sc2, g2 = (m[:, None, :] for m in adaln(c, w_mod[l], b_mod[l], 6))
        h = rms_norm(x, norm_mix_g[l]) * (1.0 + sc) + sh
        y, _, _ = hybrid_mixer(h @ w_in[l], lat_chunks, conv_q[l], conv_k[l], b_igate[l], b_fgate[l],
                               gmlp_ws[l], gmlp_bs[l], mlstm_norm_g[l], w_out[l], st_f, st_b)
        x = x + g * y
        h2 = rms_norm(x, norm_ffn_g[l]) * (1.0 + sc2) + sh2
        x = x + g2 * expert_choice_ffn(h2, w_router[l], w_gate_e[l], w_up_e[l], w_down_e[l], cap_lat)
    return rms_norm(x, final_g)


_drawn_inputs = setup_inputs


def setup_inputs(seed=0):
    import zlib

    import numpy as np

    out = dict(_drawn_inputs(seed))
    spreads = {}
    factors = {'ctx': 16.374,
     'norm_mix_g': 7.75,
     'b_igate': 64.0,
     'gmlp_bs': 8.0,
     'mlstm_norm_g': 8.0,
     'norm_ffn_g': 8.0,
     'final_g': 7.372}
    for name, (base, spread) in spreads.items():
        noise = np.random.default_rng([zlib.crc32(name.encode()), seed]).standard_normal(out[name].shape)
        drawn = base * np.exp(spread * noise) if base else spread * noise
        out[name] = jnp.asarray(drawn.astype(out[name].dtype))
    for name, factor in factors.items():
        out[name] = (out[name] * factor).astype(out[name].dtype)
    return out
```

```python
import math
from contextlib import ExitStack

import concourse.bass as bass
from concourse import mybir

ALU = mybir.AluOpType
ACT = mybir.ActivationFunctionType
AX = mybir.AxisListType
F32 = mybir.dt.float32
F32R = mybir.dt.float32r
BF16 = mybir.dt.bfloat16
U32 = mybir.dt.uint32

P = 128
EPS = 1e-6
MASKED = -1e30


def hybrid_block(nc, x, c, ctx, c_ctx, w_mod, b_mod, norm_mix_g, w_in, conv_q, conv_k, b_igate, b_fgate,
                 gmlp_ws, gmlp_bs, mlstm_norm_g, w_out, norm_ffn_g, w_router, w_gate_e, w_up_e,
                 w_down_e, final_g, out, ffn_in, stream):
    D = x.shape[2]
    T = x.shape[1]
    TC = ctx.shape[1]
    KT = D // P
    NT = T // P
    NTC = TC // P
    NE = w_router.shape[2]
    CAP = 2 * T // NE
    H = gmlp_ws.shape[1]
    W = H * P
    DE = w_gate_e.shape[3]
    ROWS = 32 + H
    TA = TC + T
    NB = NT + 1
    V1 = P + 1
    LOG_INV_SCALE = 0.5 * math.log(P)
    assert CAP == P and W == 512 and D == 1024 and H == 4

    xf = x[0]
    cf = ctx[0]
    win = w_in[0].rearrange("(k p) n -> p k n", p=P)
    wmod = w_mod[0].rearrange("(k p) n -> p k n", p=P)
    wout = w_out[0].rearrange("(k p) n -> p k n", p=P)
    Q0, O0, K0 = 2 * W, 3 * W, 4 * W
    V0, G0 = K0 + W, K0 + 2 * W

    MODC = 6 * D // W
    MOD_A = 2 * D // W
    PIECES = [("mod", i) for i in range(MOD_A)]
    PIECES += [("in", K0), ("in", V0), ("in", W), ("in", 0), ("in", Q0), ("in", O0)]
    PIECES += [("mod", i) for i in range(MOD_A, MODC)]
    PIECES += [("out", 0), ("out", 1)]
    PIECE = {p: n for n, p in enumerate(PIECES)}
    NPIECE = len(PIECES)
    MSLOT = 2
    ESLOT = 4
    GUC = DE // W
    DK = KT * W // D
    DC = DE // P // DK
    EC = 2 * GUC + DC
    assert EC % ESLOT == 0 and NPIECE % MSLOT == 0

    es = ExitStack()
    with es:
        def sb(st, name, shape, dt=F32):
            return st.enter_context(nc.sbuf_tensor(name, shape, dt))

        def sem(name):
            return es.enter_context(nc.semaphore(name))

        ring = sb(es, "ring", [P, MSLOT, KT, W])
        ident = sb(es, "ident", [P, P])
        ones = sb(es, "ones", [P, P])
        epsc = sb(es, "epsc", [P, 1])
        vcol = sb(es, "vcol", [P, P])
        scol = sb(es, "scol", [P, KT, 2])
        mod = sb(es, "mod", [P, 6 * KT, 2])
        amix = sb(es, "amix", [P, KT, 2])
        affn = sb(es, "affn", [P, KT])
        stat = sb(es, "stat", [P, 4, 16])
        g2row = sb(es, "g2row", [P, D])
        idx_f = sb(es, "idx_f", [P, NE])
        idx_u = sb(es, "idx_u", [P, NE], U32)
        gatec = sb(es, "gatec", [P, NE])

        mx = ExitStack()
        ygT = sb(mx, "ygT", [P, H, T])
        hcT = ygT[:, :, :].rearrange("p h t -> p (h t)")[:, 0:KT * TC].rearrange("p (k t) -> p k t", k=KT)
        ymT = sb(mx, "ymT", [P, H, T])
        xs = ymT[:, :, :].rearrange("p h t -> p (h t)").rearrange("p (s d) -> p s d", s=4)
        m2 = ExitStack()
        identb = sb(m2, "identb", [P, P], BF16)
        maskb = sb(m2, "maskb", [P, 2, H, P], BF16)
        zrow = sb(m2, "zrow", [ROWS, TC])
        rowU = sb(m2, "rowU", [ROWS, TA])
        rowF = sb(m2, "rowF", [ROWS, TA])
        rowB = sb(m2, "rowB", [ROWS, TA])
        rowM = sb(m2, "rowM", [ROWS, TA])
        mprev = sb(m2, "mprev", [ROWS, NB + 1])
        mprev_t = sb(m2, "mprev_t", [ROWS, NB])
        mend_t = sb(m2, "mend_t", [ROWS, NB])
        decay = sb(m2, "decay", [ROWS, NB])
        decb = sb(m2, "decb", [P, 2 * H, NB])
        colU = sb(m2, "colU", [P, NT, ROWS])
        colE = sb(m2, "colE", [P, NT, ROWS])
        colW = sb(m2, "colW", [P, NB + 1, ROWS])
        bns = sb(m2, "bns", [P, NT, H, 6])
        mv = sb(m2, "mv", [P, NT, H, 2])
        mvg = sb(m2, "mvg", [P, NT, 2])
        rsd = sb(m2, "rsd", [P, NT, H])
        floorc = sb(m2, "floorc", [ROWS, 1])
        kT = sb(m2, "kT", [P, H, T])
        kTc = sb(m2, "kTc", [P, H, TC])
        vt = sb(m2, "vt", [P, NTC + NT, H, V1])
        qv = sb(m2, "qv", [P, H * T])
        qT = qv[:, :].rearrange("p (h t) -> p h t", h=H)
        vg = qv[:, :].rearrange("p (n w) -> p n w", n=NT)
        pj = ExitStack()
        hT = sb(pj, "hT", [P, KT, T])
        raw = sb(pj, "raw", [P, T + 2])
        rawc = sb(pj, "rawc", [P, TC + 2])
        wg = sb(pj, "wg", [P, KT, P])
        gbias = sb(pj, "gbias", [P, 1])
        wsT = sb(pj, "wsT", [P, H, P])
        bsb = sb(pj, "bsb", [P, H, P])
        pj.close()
        ml = ExitStack()
        hs = sb(ml, "hs", [P, NT, H, P])
        sel = sb(ml, "sel", [P, 2 * H, P])
        state = sb(ml, "state", [P, 2, H, V1])
        kt = sb(ml, "kt", [P, 2, H, P])
        et = sb(ml, "et", [P, 2, H, P])
        st = sb(ml, "st", [P, 2, H, P])
        qs = sb(ml, "qs", [P, 2, H, P])
        vw = sb(ml, "vw", [P, 2, H, V1])
        den = sb(ml, "den", [P, 2, 3, H])
        ml.close()
        m2.close()
        op = ExitStack()
        grow = sb(op, "grow", [P, D])
        a2row = sb(op, "a2row", [P, D])
        b2row = sb(op, "b2row", [P, D])
        wr = sb(op, "wr", [P, KT, NE])
        xr = sb(op, "xr", [P, 2, D])
        x2 = sb(op, "x2", [P, 2, D])
        h2 = sb(op, "h2", [P, 2, D])
        h2T = sb(op, "h2T", [P, 2, KT, P])
        sq = sb(op, "sq", [P, D])
        aff = sb(op, "aff", [P, NT, NE])
        srt = sb(op, "srt", [P, 2, NT])
        affT = sb(op, "affT", [NE, T])
        topv = sb(op, "topv", [NE, CAP])
        topi = sb(op, "topi", [NE, CAP], U32)
        topf = sb(op, "topf", [NE, CAP])
        op.close()
        mx.close()

        xe = sb(es, "xe", [P, D])
        xeh = sb(es, "xeh", [P, KT, P], F32R)
        xel = sb(es, "xel", [P, KT, P], F32R)
        yw = sb(es, "yw", [P, D])
        wh = sb(es, "wh", [P, 4, KT * W // 2], F32R)
        wl = sb(es, "wl", [P, 4, KT * W // 2], F32R)
        hidh = sb(es, "hidh", [P, DE // P, P], F32R)
        hidl = sb(es, "hidl", [P, DE // P, P], F32R)
        ring2 = sb(es, "ring2", [P, ESLOT - MSLOT, KT, W])
        sil = sb(es, "sil", [P, 2, W])
        hid = sb(es, "hid", [P, 2, W])
        idx_e = sb(es, "idx_e", [P, 2], U32)
        gate_e = sb(es, "gate_e", [P, 2])
        fgrow = sb(es, "fgrow", [P, D])

        ps = es.enter_context(nc.psum_tensor("ps", [P, 8, 512], F32))


        consts_in = sem("consts_in")
        pool_step = sem("pool_step")
        pool_turn = sem("pool_turn")
        act_step = sem("act_step")
        dve_step = sem("dve_step")
        vecs_in = sem("vecs_in")
        ws_in = sem("ws_in")
        bs_in = sem("bs_in")
        gates_in = sem("gates_in")
        x_in = [sem(f"x_in{i}") for i in range(4)]
        piece_in = [sem(f"piece_in{i}") for i in range(MSLOT)]
        piece_used = sem("piece_used")
        ss_ready = sem("ss_ready")
        xn_ready = sem("xn_ready")
        xt_ready = sem("xt_ready")
        xt_free = sem("xt_free")
        vec_t = sem("vec_t")
        vcol_ready = sem("vcol_ready")
        scol_ready = sem("scol_ready")
        ws_t = sem("ws_t")
        wsT_ready = sem("wsT_ready")
        h_ready = sem("h_ready")
        pj_done = sem("pj_done")
        pj_free = sem("pj_free")
        nab_ready = sem("nab_ready")
        lnf_ready = sem("lnf_ready")
        convk_done = sem("convk_done")
        convq_done = sem("convq_done")
        k_ready = sem("k_ready")
        q_ready = sem("q_ready")
        rowU_ready = sem("rowU_ready")
        colU_t = sem("colU_t")
        colU_ready = sem("colU_ready")
        rowx_ready = sem("rowx_ready")
        roww_ready = sem("roww_ready")
        rowe_ready = sem("rowe_ready")
        cols_t = sem("cols_t")
        cols_ready = sem("cols_ready")
        vgstat_ready = sem("vgstat_ready")
        vgroot_ready = sem("vgroot_ready")
        vln_ready = sem("vln_ready")
        s_done = sem("s_done")
        s_free = sem("s_free")
        sel_ready = sem("sel_ready")
        ckt_t = sem("ckt_t")
        ckt_c = sem("ckt_c")
        cvw_done = sem("cvw_done")
        cst_done = sem("cst_done")
        cst_ready = sem("cst_ready")
        kt_t = sem("kt_t")
        kt_c = sem("kt_c")
        m_done = sem("m_done")
        e_done = sem("e_done")
        qk_done = sem("qk_done")
        qs_done = sem("qs_done")
        st_done = sem("st_done")
        vw_done = sem("vw_done")
        num_done = sem("num_done")
        abs_done = sem("abs_done")
        h_done = sem("h_done")
        su_done = sem("su_done")
        state_up = sem("state_up")
        hstat_ready = sem("hstat_ready")
        hroot_ready = sem("hroot_ready")
        hn_ready = sem("hn_ready")
        hn_t = sem("hn_t")
        ym_ready = sem("ym_ready")
        dg_ready = sem("dg_ready")
        row_t = sem("row_t")
        row_c = sem("row_c")
        wr_in = sem("wr_in")
        xr_in = [sem(f"xr_in{i}") for i in range(2)]
        op_done = sem("op_done")
        op_free = sem("op_free")
        x2_ready = sem("x2_ready")
        ss2_ready = sem("ss2_ready")
        h2_ready = sem("h2_ready")
        x2_out = [sem(f"x2_out{i}") for i in range(2)]
        h2_out = [sem(f"h2_out{i}") for i in range(2)]
        h2_t = sem("h2_t")
        h2_c = sem("h2_c")
        rt_done = sem("rt_done")
        ex_arg = sem("ex_arg")
        ex_done = sem("ex_done")
        aff_ready = sem("aff_ready")
        aff_t = sem("aff_t")
        top_ready = sem("top_ready")
        top_t = sem("top_t")
        idx_ready = sem("idx_ready")
        fg_in = sem("fg_in")
        e_in = [sem(f"e_in{i}") for i in range(ESLOT)]
        hi_done = sem("hi_done")
        lo_done = sem("lo_done")
        mm_done = sem("mm_done")
        idxg_ready = sem("idxg_ready")
        xe_in = sem("xe_in")
        xe_t = sem("xe_t")
        xeh_done = sem("xeh_done")
        xel_done = sem("xel_done")
        sil_done = sem("sil_done")
        hid_done = sem("hid_done")
        hid_t = sem("hid_t")
        hidh_done = sem("hidh_done")
        hidl_done = sem("hidl_done")
        yw_done = sem("yw_done")
        added = sem("added")
        gate_ready = sem("gate_ready")
        fin_in = [sem(f"fin_in{i}") for i in range(NT)]
        froot_ready = sem("froot_ready")
        fin_ready = sem("fin_ready")
        out_in = sem("out_in")

        def chain(eng, s):
            n = [0]

            def link(ins):
                n[0] += 1
                ins.then_inc(s, 1)
                eng.wait_ge(s, n[0])
            return link

        def two(a, b):
            return ps[:, a:b, :].rearrange("p b n -> p (b n)")

        whv = [wh[:, i, :] for i in range(4)]
        wlv = [wl[:, i, :] for i in range(4)]
        finv = ring2[:, :, :, :].rearrange("p s k n -> p (s k n)").rearrange("p (t d) -> p t d", t=NT)

        def eview(m):
            i = m // 2 % ESLOT
            v = (ring[:, i] if i < MSLOT else ring2[:, i - MSLOT]).rearrange("p k n -> p (k n)")
            n = KT * W // 2
            return v[:, m % 2 * n:(m % 2 + 1) * n]

        def landed_piece(eng, n):
            eng.wait_ge(piece_in[n % MSLOT], 16 * (n // MSLOT + 1))

        VROW = {}
        at = 0
        for name, n in (("b_mod", 6 * KT), ("c", KT), ("c_ctx", KT), ("mix_g", KT), ("ffn_g", KT),
                        ("conv_q", 3 * H), ("conv_k", 3 * H), ("mlstm_g", H)):
            VROW[name] = at
            at += n
        NVEC = at
        vecs = g2row[:, 0:P]
        wsraw = g2row[:, P:P + H * P].rearrange("p (h q) -> p h q", h=H)

        HALF = 512
        NH2 = T // HALF
        GROUPS = [("g", 0, 0)] + [("g", 1, h) for h in range(NH2)]
        for ct in range(H):
            GROUPS += [("kc", ct, 0)] + [("k", ct, h) for h in range(NH2)]
        GROUPS += [("vc", n, 0) for n in range(NTC)] + [("v", n, 0) for n in range(NT)]
        GROUPS += [("vg", n, 0) for n in range(NT)]
        for kind in "uoq":
            GROUPS += [(kind, ct, h) for ct in range(H) for h in range(NH2)]
        GAT = {g: n for n, g in enumerate(GROUPS)}
        PIECE_OF = {"kc": ("in", K0), "k": ("in", K0), "vc": ("in", V0), "v": ("in", V0), "vg": ("in", W),
                    "u": ("in", 0), "o": ("in", O0), "q": ("in", Q0)}

        def block_of(d, j):
            if j == 0:
                return 0, TC
            c0 = j - 1 if d == 0 else NT - j
            return TC + c0 * P, TC + (c0 + 1) * P

        def run(t, d, j):
            a, b = block_of(d, j)
            v = t[32 * d:32 * d + H, a:b]
            return v if d == 0 else v[:, ::-1]

        STEPS = [(j, d) for j in range(NT) for d in range(2)]
        NS = len(STEPS)
        NSU = NS - 2

        def chunk(s):
            j, d = STEPS[s]
            return j if d == 0 else NT - 1 - j

        CTXBANKS = ((4, 5), (6, 1))

        block = es.enter_context(nc.Block())

        @block.gpsimd
        def _(pool):
            link = chain(pool, pool_step)
            for t in range(4):
                src = cf[t * P:(t + 1) * P, :] if t < NTC else xf[(t - NTC) * P:(t - NTC + 1) * P, :]
                pool.dma_start(xs[:, t, :], src).then_inc(x_in[t], 16)
            link(pool.memset(ident[:], 0.0))
            link(pool.affine_select(out=ident[:], in_=ident[:], compare_op=ALU.not_equal, fill=1.0, base=0,
                                    pattern=[[-1, P]], channel_multiplier=1))
            pool.memset(ones[:], 1.0)
            pool.memset(epsc[:], EPS)
            pool.tensor_copy(identb[:], ident[:])
            pool.memset(floorc[:], LOG_INV_SCALE)
            pool.memset(zrow[:], 0.0)
            pool.memset(rowB[:], 0.0)
            pool.memset(rowM[:], 0.0)
            pool.memset(mprev[:], 0.0)
            pool.memset(mend_t[:], 0.0)
            pool.memset(mprev_t[:], 0.0)
            pool.memset(raw[:, 0:1], 0.0)
            pool.memset(raw[:, T + 1:T + 2], 0.0)
            pool.memset(rawc[:, 0:1], 0.0)
            pool.memset(rawc[:, TC + 1:TC + 2], 0.0)
            pool.memset(vt[:, :, :, P:V1], 1.0)
            link(pool.memset(gbias[:], 0.0))
            link(pool.memset(wg[:], 0.0))
            link(pool.memset(maskb[:], 0.0))
            for d, sign in ((0, 1), (1, -1)):
                link(pool.affine_select(out=maskb[:, d], in_=maskb[:, d], compare_op=ALU.is_ge, fill=MASKED,
                                        base=0, pattern=[[0, H], [sign, P]], channel_multiplier=-sign))
            pool.sem_inc(consts_in, 1)
            for n in range(4):
                src = w_in[0][:, G0 + H * n:G0 + H * (n + 1)].rearrange("(k p) n -> p k n", p=P)
                pool.dma_start(wg[:, :, 32 * n:32 * n + H], src).then_inc(gates_in, 16)
                b = (b_igate, b_fgate)[n // 2][0, n % 2].rearrange("(h a) -> h a", a=1)
                pool.dma_start(gbias[32 * n:32 * n + H, :], b).then_inc(gates_in, 16)
            pool.dma_start(bsb[:], gmlp_bs[0].partition_broadcast(P)).then_inc(bs_in, 16)
            for t in range(4, NTC + NT):
                pool.wait_ge(xt_ready, t - 3)
                pool.dma_start(xs[:, t % 4, :], xf[(t - NTC) * P:(t - NTC + 1) * P, :]).then_inc(x_in[t % 4], 16)
            pool.wait_ge(pj_done, len(GROUPS))
            pool.wait_ge(q_ready, H)
            pool.wait_ge(s_free, NT)
            link(pool.memset(sel[:], 0.0))
            for d in range(2):
                for h in range(H):
                    last = pool.affine_select(out=sel[:, H * d + h], in_=sel[:, H * d + h],
                                              compare_op=ALU.not_equal, fill=1.0, base=-(32 * d + h),
                                              pattern=[[0, P]], channel_multiplier=1)
            link(last)
            pool.sem_inc(sel_ready, 1)
            pool.wait_ge(ym_ready, 1)
            pool.dma_start(wr[:], w_router[0].rearrange("(k p) n -> p k n", p=P)).then_inc(wr_in, 16)
            for t in range(NT):
                if t >= 2:
                    pool.wait_ge(x2_ready, t - 1)
                pool.dma_start(xr[:, t % 2, :], xf[t * P:(t + 1) * P, :]).then_inc(xr_in[t % 2], 16)
            pool.wait_ge(idx_ready, 1)
            pool.dma_start(fgrow[:], final_g.partition_broadcast(P)).then_inc(fg_in, 16)
            for i in range(2):
                pool.wait_ge(h2_out[i], 16 * (NT // 2))
                pool.wait_ge(x2_out[i], 16 * (NT // 2))

            def gather(e):
                pool.sem_inc(pool_turn, 1)
                pool.indirect_dma_start(
                    out=xe[:, :], out_offset=None, in_=ffn_in,
                    in_offset=bass.IndirectOffsetOnAxis(ap=idx_e[:, 0:1], axis=0)).then_inc(xe_in, 16)

            def scatter(e):
                pool.wait_ge(yw_done, e + 1)
                pool.sem_inc(pool_turn, 1)
                pool.indirect_dma_start(
                    out=stream, out_offset=bass.IndirectOffsetOnAxis(ap=idx_e[:, 1:2], axis=0),
                    in_=yw[:, :], in_offset=None, compute_op=ALU.add).then_inc(added, 16)

            pool.wait_ge(idxg_ready, 1)
            gather(0)
            pool.wait_ge(idxg_ready, 2)
            pool.wait_ge(xe_t, 2)
            gather(1)
            with pool.Fori(1, NE - 1) as e:
                scatter(e - 1)
                pool.wait_ge(idxg_ready, e + 2)
                pool.wait_ge(xe_t, 2 * e + 2)
                gather(e + 1)
                pool.wait_ge(added, 16 * e)
            scatter(NE - 2)
            pool.wait_ge(added, 16 * (NE - 1))
            scatter(NE - 1)
            pool.wait_ge(added, 16 * NE)

        @block.sync
        def _(sp):
            for n, (kind, c0) in enumerate(PIECES):
                if n >= MSLOT:
                    k0, i0 = PIECES[n - MSLOT]
                    if k0 == "mod":
                        sp.wait_ge(piece_used, i0 + 1)
                    else:
                        sp.wait_ge(pj_done, 1 + max(g for g, v in enumerate(GROUPS) if PIECE_OF.get(v[0]) == (k0, i0)))
                src = {"mod": lambda: wmod[:, :, c0 * W:(c0 + 1) * W], "in": lambda: win[:, :, c0:c0 + W],
                       "out": lambda: wout[:, :, c0 * W:(c0 + 1) * W]}[kind]()
                sp.dma_start(ring[:, n % MSLOT], src).then_inc(piece_in[n % MSLOT], 16)

            def eslot(m):
                return ring[:, m] if m < MSLOT else ring2[:, m - MSLOT]

            def load(e, m):
                if m < 2 * GUC:
                    w, c0 = (w_gate_e, w_up_e)[m % 2], m // 2 * W
                    src = w[0][e, :, c0:c0 + W].rearrange("(k p) n -> p k n", p=P)
                    dst = eslot(m % ESLOT)
                else:
                    r0 = (m - 2 * GUC) * DK * P
                    src = w_down_e[0][e, r0:r0 + DK * P, :].rearrange("(k p) n -> p k n", p=P)
                    dst = eslot(m % ESLOT).rearrange("p k n -> p (k n)").rearrange("p (k n) -> p k n", k=DK)
                sp.dma_start(dst, src).then_inc(e_in[m % ESLOT], 16)

            for m in range(EC):
                if m < MSLOT:
                    sp.wait_ge(op_done, NT)
                elif m < ESLOT:
                    sp.wait_ge(ym_ready, 1)
                else:
                    sp.wait_ge(lo_done, 2 * (m - ESLOT + 1))
                load(0, m)
            with sp.Fori(1, NE) as e:
                for m in range(EC):
                    sp.wait_ge(lo_done, e * (2 * EC) + 2 * (m - ESLOT + 1))
                    load(e, m)
            sp.wait_ge(lo_done, 2 * EC * NE)
            sp.wait_ge(added, 16 * NE)
            for t in range(NT):
                sp.dma_start(finv[:, t, :], stream[t * P:(t + 1) * P, :]).then_inc(fin_in[t], 16)
            for t in range(NT):
                sp.wait_ge(fin_ready, t + 1)
                sp.dma_start(out[0][t * P:(t + 1) * P, :], finv[:, t, :]).then_inc(out_in, 16)
            sp.wait_ge(out_in, 16 * NT)

        @block.scalar
        def _(act):
            link = chain(act, act_step)
            rows = {"b_mod": b_mod[0], "c": c[0], "c_ctx": c_ctx, "mix_g": norm_mix_g[0], "ffn_g": norm_ffn_g[0],
                    "conv_q": conv_q[0].rearrange("j n -> (j n)"), "conv_k": conv_k[0].rearrange("j n -> (j n)"),
                    "mlstm_g": mlstm_norm_g[0]}
            for name, v in rows.items():
                n = v.shape[0] // P
                act.dma_start(vecs[VROW[name]:VROW[name] + n, :], v.rearrange("(r p) -> r p", p=P)).then_inc(vecs_in, 16)
            act.dma_start(wsraw[:], gmlp_ws[0].rearrange("h p q -> p h q")).then_inc(ws_in, 16)
            act.wait_ge(consts_in, 1)

            def norm_copy(t):
                act.wait_ge(xt_ready, t + 1)
                dst = hcT[:, :, t * P:(t + 1) * P] if t < NTC else hT[:, :, (t - NTC) * P:(t - NTC + 1) * P]
                b = 2 * (t % 2)
                act.activation(dst, two(b, b + 2).rearrange("p (k t) -> p k t", k=KT), ACT.Copy).then_inc(xt_free, 1)

            for t in range(NTC + NT):
                act.wait_ge(x_in[t % 4], 16 * (t // 4 + 1))
                if t >= 1:
                    act.wait_ge(ss_ready, t)
                link(act.activation(raw[:, 1:1 + D], xs[:, t % 4, :], ACT.Square, accum_out=stat[:, 0, t:t + 1]))
                act.activation(stat[:, 1, t:t + 1], stat[:, 0, t:t + 1], ACT.Sqrt, bias=epsc[:],
                               scale=1.0 / D).then_inc(ss_ready, 1)
                if t >= 1:
                    norm_copy(t - 1)
            norm_copy(NTC + NT - 1)
            act.wait_ge(vcol_ready, 1)
            act.activation(scol[:].rearrange("p k c -> p c k"),
                           vcol[:, VROW["c"]:VROW["c"] + 2 * KT].rearrange("p (c k) -> p c k", c=2),
                           ACT.Silu).then_inc(scol_ready, 1)
            act.wait_ge(ws_t, 1)
            act.activation(wsT[:], ps[:, 5, :].rearrange("p (h q) -> p h q", h=H), ACT.Copy).then_inc(wsT_ready, 1)

            def take(g, dst, src, f=ACT.Copy):
                act.wait_ge(pj_done, g + 1)
                act.activation(dst, src, f).then_inc(pj_free, 1)

            act.wait_ge(gates_in, 8 * 16)
            for kind, blk, h in GROUPS[0:1 + NH2]:
                g = GAT[kind, blk, h]
                a, n = (0, TC) if blk == 0 else (TC + h * HALF, HALF)
                act.wait_ge(pj_done, g + 1)
                act.activation(rowU[:, a:a + n], ps[0:ROWS, g % 4, 0:n], ACT.Identity, bias=gbias[0:ROWS, :])
                act.activation(rowF[:, a:a + n], ps[64:64 + ROWS, g % 4, 0:n], ACT.Identity,
                               bias=gbias[64:64 + ROWS, :]).then_inc(pj_free, 1)
            act.wait_ge(nab_ready, 1)
            link(act.activation(rowB[:], rowB[:], ACT.Exp))
            act.activation(rowB[:], rowB[:], ACT.Ln, bias=1.0).then_inc(lnf_ready, 1)
            for ct in range(H):
                if ct >= 1:
                    act.wait_ge(convk_done, ct)
                g = GAT["kc", ct, 0]
                take(g, rawc[:, 1:1 + TC], ps[:, g % 4, 0:TC])
                for h in range(NH2):
                    g = GAT["k", ct, h]
                    take(g, raw[:, 1 + h * HALF:1 + (h + 1) * HALF], ps[:, g % 4, :])
                if ct >= 1:
                    act.activation(kTc[:, ct - 1], kTc[:, ct - 1], ACT.Silu)
                    act.activation(kT[:, ct - 1], kT[:, ct - 1], ACT.Silu).then_inc(k_ready, 1)
            act.wait_ge(convk_done, H)
            act.activation(kTc[:, H - 1], kTc[:, H - 1], ACT.Silu)
            act.activation(kT[:, H - 1], kT[:, H - 1], ACT.Silu).then_inc(k_ready, 1)
            for n in range(NTC + NT):
                g = GAT[("vc", n, 0) if n < NTC else ("v", n - NTC, 0)]
                take(g, vt[:, n, :, 0:P], ps[:, g % 4, :].rearrange("p (h d) -> p h d", h=H))
            act.wait_ge(rowx_ready, 1)
            act.activation(decay[:], decay[:], ACT.Exp)
            act.activation(rowF[:, TC:TA], rowF[:, TC:TA], ACT.Exp)
            act.activation(rowB[:, TC:TA], rowB[:, TC:TA], ACT.Exp, scale=-1.0, bias=floorc[:]).then_inc(rowe_ready, 1)
            act.wait_ge(roww_ready, 1)
            act.activation(rowU[:], rowU[:], ACT.Exp).then_inc(rowe_ready, 1)
            for n in range(NT):
                g = GAT["vg", n, 0]
                take(g, vg[:, n, :], ps[:, g % 4, :], ACT.Gelu_apprx_tanh)
            for ct in range(H):
                for h in range(NH2):
                    g = GAT["u", ct, h]
                    take(g, ygT[:, ct, h * HALF:(h + 1) * HALF], ps[:, g % 4, :], ACT.Gelu_apprx_tanh)
            act.wait_ge(vgstat_ready, 1)
            act.activation(rsd[:, :, 0], mvg[:, :, 1], ACT.Sqrt, bias=epsc[:]).then_inc(vgroot_ready, 1)
            for ct in range(H):
                for h in range(NH2):
                    g = GAT["o", ct, h]
                    take(g, ymT[:, ct, h * HALF:(h + 1) * HALF], ps[:, g % 4, :], ACT.Sigmoid)
            act.wait_ge(s_free, NT)
            for ct in range(H):
                if ct >= 1:
                    act.wait_ge(convq_done, ct)
                for h in range(NH2):
                    g = GAT["q", ct, h]
                    take(g, raw[:, 1 + h * HALF:1 + (h + 1) * HALF], ps[:, g % 4, :])
                if ct >= 1:
                    act.activation(qT[:, ct - 1], qT[:, ct - 1], ACT.Silu).then_inc(q_ready, 1)
            act.wait_ge(convq_done, H)
            act.activation(qT[:, H - 1], qT[:, H - 1], ACT.Silu).then_inc(q_ready, 1)

            for n in range(NTC):
                act.wait_ge(ckt_t, n + 1)
                act.activation(kt[:, n], ps[:, 2 * n, :].rearrange("p (h d) -> p h d", h=H), ACT.Copy).then_inc(ckt_c, 1)
            act.wait_ge(colU_ready, 1)
            for s in range(NS + 1):
                if s < NS:
                    d, c0 = STEPS[s][1], chunk(s)
                    if s < NSU:
                        act.wait_ge(kt_t, s + 1)
                        act.wait_ge(cst_done, 2)
                        if s >= 2:
                            act.wait_ge(su_done, s - 1)
                        act.activation(kt[:, s % 2], ps[:, 0, :].rearrange("p (h d) -> p h d", h=H),
                                       ACT.Copy).then_inc(kt_c, 1)
                    act.wait_ge(m_done, s + 1)
                    if s >= 2:
                        act.wait_ge(st_done, s - 1)
                    for h in range(H):
                        last = act.activation(et[:, s % 2, h], ps[:, 2, h * P:(h + 1) * P], ACT.Exp,
                                              bias=colU[:, c0, 32 * d + h:32 * d + h + 1])
                    last.then_inc(e_done, 1)
                if s >= 1:
                    act.wait_ge(num_done, s)
                    if s >= 3:
                        act.wait_ge(h_done, s - 2)
                    act.activation(den[:, (s - 1) % 2, 0, :].rearrange("p (a b) -> p a b", a=2),
                                   ps[:, 4:6, 0:2 * V1].rearrange("p a (b v) -> p a b v", v=V1)[:, :, :, P],
                                   ACT.Abs).then_inc(abs_done, 1)
            act.wait_ge(hstat_ready, 1)
            act.activation(rsd[:], mv[:, :, :, 1], ACT.Sqrt, bias=epsc[:]).then_inc(hroot_ready, 1)

            act.wait_ge(ym_ready, 1)
            for r, dst in enumerate((grow, a2row, b2row, g2row)):
                act.wait_ge(row_t, r + 1)
                b = 4 + 2 * (r % 2)
                act.activation(dst[:], two(b, b + 2), ACT.Copy).then_inc(row_c, 1)

            def feature_copy(t):
                act.wait_ge(h2_t, t + 1)
                if t >= 2:
                    act.wait_ge(rt_done, t - 1)
                act.activation(h2T[:, t % 2], two(4, 6).rearrange("p (k t) -> p k t", k=KT),
                               ACT.Copy).then_inc(h2_c, 1)

            for t in range(NT):
                act.wait_ge(x2_ready, t + 1)
                act.dma_start(stream[t * P:(t + 1) * P, :], x2[:, t % 2, :]).then_inc(x2_out[t % 2], 16)
                if t >= 1:
                    act.wait_ge(ss2_ready, t)
                link(act.activation(sq[:], x2[:, t % 2, :], ACT.Square, accum_out=stat[:, 0, t:t + 1]))
                act.activation(stat[:, 1, t:t + 1], stat[:, 0, t:t + 1], ACT.Sqrt, bias=epsc[:],
                               scale=1.0 / D).then_inc(ss2_ready, 1)
                if t >= 1:
                    act.wait_ge(h2_ready, t)
                    act.dma_start(ffn_in[(t - 1) * P:t * P, :], h2[:, (t - 1) % 2, :]).then_inc(h2_out[(t - 1) % 2], 16)
                    feature_copy(t - 1)
            act.wait_ge(h2_ready, NT)
            act.dma_start(ffn_in[(NT - 1) * P:NT * P, :], h2[:, (NT - 1) % 2, :]).then_inc(h2_out[(NT - 1) % 2], 16)
            feature_copy(NT - 1)
            act.wait_ge(ex_arg, 1)
            act.activation(aff[:], aff[:], ACT.Exp).then_inc(ex_done, 1)

            act.wait_ge(idx_ready, 1)

            def features_high(e, r):
                act.wait_ge(xe_t, 2 * e + r + 1)
                hk = KT // 2
                act.activation(xeh[:, r * hk:(r + 1) * hk], ps[:, 7, :].rearrange("p (k t) -> p k t", k=hk),
                               ACT.Copy).then_inc(xeh_done, 1)

            def expert(e, first, last):
                for m in range(2 * EC):
                    if m % 2 == 0:
                        pm = m // 2
                        act.wait_ge(e_in[pm % ESLOT], e * (16 * EC // ESLOT) + 16 * (pm // ESLOT + 1))
                    if not first or m >= 4:
                        act.wait_ge(mm_done, e * (2 * EC) + m - 3)
                    act.activation(whv[m % 4], eview(m), ACT.Copy).then_inc(hi_done, 1)
                    if m % 4 == 3 and 7 <= m < 4 * GUC + 4:
                        q = (m - 7) // 4
                        act.wait_ge(mm_done, e * (2 * EC) + 4 * q + 4)
                        if not first or q >= 2:
                            act.wait_ge(hid_done, e * GUC + q - 1)
                        act.activation(sil[:, q % 2], ps[:, 2 * (q % 2), :], ACT.Silu).then_inc(sil_done, 1)
                    if m % 4 == 1 and 9 <= m < 4 * GUC + 6:
                        q = (m - 9) // 4
                        act.wait_ge(hid_t, e * GUC + q + 1)
                        act.activation(hidh[:, 4 * q:4 * q + 4], ps[:, 4, :].rearrange("p (k t) -> p k t", k=4),
                                       ACT.Copy).then_inc(hidh_done, 1)
                    if not last and m in (21, 23):
                        features_high(e + 1, (m - 21) // 2)

            features_high(0, 0)
            features_high(0, 1)
            expert(0, True, False)
            with act.Fori(1, NE - 1) as e:
                expert(e, False, False)
            expert(NE - 1, False, True)

            for t in range(NT):
                act.wait_ge(fin_in[t], 16)
                if t >= 1:
                    act.wait_ge(froot_ready, t)
                else:
                    act.wait_ge(hid_done, NE * GUC)
                link(act.activation(sil[:].rearrange("p a n -> p (a n)"), finv[:, t, :], ACT.Square,
                                    accum_out=stat[:, 0, t:t + 1]))
                act.activation(stat[:, 1, t:t + 1], stat[:, 0, t:t + 1], ACT.Sqrt, bias=epsc[:],
                               scale=1.0 / D).then_inc(froot_ready, 1)

        @block.tensor
        def _(pe):
            def mm(o, l, r, start, stop):
                return pe.matmul(o, l, r, start=start, stop=stop)

            pe.wait_ge(consts_in, 1)
            pe.wait_ge(vecs_in, 16 * 8)
            pe.transpose(ps[:, 4, 0:NVEC], vecs[0:NVEC, :], ident[0:NVEC, 0:NVEC]).then_inc(vec_t, 1)
            pe.wait_ge(ws_in, 16)
            for h in range(H):
                last = pe.transpose(ps[:, 5, h * P:(h + 1) * P], wsraw[:, h], ident[:])
            last.then_inc(ws_t, 1)
            for t in range(NTC + NT):
                pe.wait_ge(xn_ready, t + 1)
                if t >= 2:
                    pe.wait_ge(xt_free, t - 1)
                for k in range(KT):
                    last = pe.transpose(ps[:, 2 * (t % 2) + k // 4, k % 4 * P:(k % 4 + 1) * P],
                                        xs[:, t % 4, k * P:(k + 1) * P], ident[:])
                last.then_inc(xt_ready, 1)

            def modulation(i):
                n = PIECE["mod", i]
                landed_piece(pe, n)
                for ct in range(W // P):
                    j = i * (W // P) + ct
                    for k in range(KT):
                        last = mm(ps[:, 7, 2 * j:2 * j + 2], ring[:, n % MSLOT, k, ct * P:(ct + 1) * P],
                                  scol[:, k, :], k == 0, k == KT - 1)
                last.then_inc(piece_used, 1)

            pe.wait_ge(scol_ready, 1)
            for i in range(MOD_A):
                modulation(i)
            pe.wait_ge(h_ready, 1)
            pe.wait_ge(gates_in, 8 * 16)
            pe.wait_ge(xt_free, NTC + NT)

            def group(g):
                kind, i, h = GROUPS[g]
                if g >= 4:
                    pe.wait_ge(pj_free, g - 3)
                o = ps[:, g % 4, :]
                if kind == "g":
                    src, a, n = (hcT, 0, TC) if i == 0 else (hT, h * HALF, HALF)
                    for k in range(KT):
                        last = mm(o[:, 0:n], wg[:, k, :], src[:, k, a:a + n], k == 0, k == KT - 1)
                    last.then_inc(pj_done, 1)
                    return
                piece = PIECE[PIECE_OF[kind]]
                w = ring[:, piece % MSLOT]
                first = GROUPS[g - 1][0] == "g" or PIECE_OF[GROUPS[g - 1][0]] != PIECE_OF[kind]
                if first:
                    landed_piece(pe, piece)
                for k in range(KT):
                    if kind in ("vc", "v", "vg"):
                        src = hcT if kind == "vc" else hT
                        last = mm(o, src[:, k, i * P:(i + 1) * P], w[:, k, :], k == 0, k == KT - 1)
                    elif kind == "kc":
                        last = mm(o[:, 0:TC], w[:, k, i * P:(i + 1) * P], hcT[:, k, :], k == 0, k == KT - 1)
                    else:
                        last = mm(o, w[:, k, i * P:(i + 1) * P], hT[:, k, h * HALF:(h + 1) * HALF],
                                  k == 0, k == KT - 1)
                last.then_inc(pj_done, 1)

            for g in range(GAT["vg", 0, 0]):
                group(g)
            pe.wait_ge(rowU_ready, 1)
            for n in range(NT):
                last = pe.transpose(ps[:, 4, n * ROWS:(n + 1) * ROWS], rowU[:, TC + n * P:TC + (n + 1) * P],
                                    ident[0:ROWS, 0:ROWS])
            last.then_inc(colU_t, 1)
            for g in range(GAT["vg", 0, 0], GAT["q", 0, 0]):
                group(g)
            pe.wait_ge(vln_ready, 1)
            pe.wait_ge(wsT_ready, 1)
            for n in range(NT):
                if n >= 2:
                    pe.wait_ge(s_free, n - 1)
                for h in range(H):
                    last = mm(ps[:, 6 + n % 2, h * P:(h + 1) * P], vg[:, n, h * P:(h + 1) * P], wsT[:, h], True, True)
                last.then_inc(s_done, 1)
            pe.wait_ge(rowe_ready, 2)
            pe.wait_ge(colU_ready, 1)
            for n in range(NT):
                pe.transpose(ps[:, 4, n * ROWS:(n + 1) * ROWS], rowB[:, TC + n * P:TC + (n + 1) * P],
                             ident[0:ROWS, 0:ROWS])
            for n in range(NTC + NT):
                last = pe.transpose(ps[:, 5, n * ROWS:(n + 1) * ROWS], rowU[:, n * P:(n + 1) * P],
                                    ident[0:ROWS, 0:ROWS])
            last.then_inc(cols_t, 1)
            for g in range(GAT["q", 0, 0], len(GROUPS)):
                group(g)
            pe.wait_ge(sel_ready, 1)
            pe.wait_ge(s_free, NT)
            for r in range(2 * H):
                last = mm(ps[:, 7, r * NB:(r + 1) * NB], sel[0:ROWS, r], decay[:], True, True)
            last.then_inc(cols_t, 1)

            pe.wait_ge(k_ready, H)
            pe.wait_ge(cols_ready, 1)
            pe.wait_ge(pj_free, len(GROUPS))
            for n in range(NTC):
                for h in range(H):
                    last = pe.transpose(ps[:, 2 * n, h * P:(h + 1) * P], kTc[:, h, n * P:(n + 1) * P], ident[:])
                last.then_inc(ckt_t, 1)
            pe.wait_ge(ckt_c, NTC)
            for d in range(2):
                pe.wait_ge(cvw_done, d + 1)
                for h in range(H):
                    o = ps[:, CTXBANKS[d][h // 2], h % 2 * V1:(h % 2 + 1) * V1]
                    for n in range(NTC):
                        last = mm(o, kt[:, n, h], vw[:, n, h], n == 0, n == NTC - 1)
                last.then_inc(cst_done, 1)

            def front(s):
                d, c0 = STEPS[s][1], chunk(s)
                a, b = c0 * P, (c0 + 1) * P
                if s < NSU:
                    if s >= 2:
                        pe.wait_ge(state_up, s - 1)
                    if s >= 1:
                        pe.wait_ge(kt_c, s)
                    for h in range(H):
                        last = pe.transpose(ps[:, 0, h * P:(h + 1) * P], kT[:, h, a:b], ident[:])
                    last.then_inc(kt_t, 1)
                if s >= 1:
                    pe.wait_ge(e_done, s)
                mm(ps[:, 2, :], identb[:], maskb[:, d].rearrange("p h t -> p (h t)"), True, False)
                for h in range(H):
                    last = mm(ps[:, 2, h * P:(h + 1) * P], sel[0:ROWS, H * d + h], rowM[:, TC + a:TC + b],
                              False, h == H - 1)
                last.then_inc(m_done, 1)
                if s >= 1:
                    pe.wait_ge(qs_done, s)
                    pe.wait_ge(st_done, s)
                for h in range(H):
                    mm(ps[:, 3, h * P:(h + 1) * P], sel[0:ROWS, H * d + h], rowF[:, TC + a:TC + b], True, True)
                for h in range(H):
                    last = mm(ps[:, 1, h * P:(h + 1) * P], kT[:, h, a:b], qT[:, h, a:b], True, True)
                last.then_inc(qk_done, 1)

            def back(s):
                d, c0 = STEPS[s][1], chunk(s)
                pe.wait_ge(st_done, s + 1)
                pe.wait_ge(qs_done, s + 1)
                if s >= 2:
                    pe.wait_ge(state_up, s - 1)
                if s >= 1:
                    pe.wait_ge(h_done, s)
                for h in range(H):
                    o = ps[:, 4 + h // 2, h % 2 * V1:(h % 2 + 1) * V1]
                    mm(o, st[:, s % 2, h], vt[:, NTC + c0, h], True, False)
                    last = mm(o, qs[:, s % 2, h], state[:, d, h], False, True)
                last.then_inc(num_done, 1)
                if s >= NSU:
                    return
                pe.wait_ge(kt_c, min(s + 2, NSU))
                pe.wait_ge(vw_done, s + 1)
                if s >= 1:
                    pe.wait_ge(state_up, s)
                for h in range(H):
                    o = ps[:, (6, 0)[h // 2], h % 2 * V1:(h % 2 + 1) * V1]
                    last = mm(o, kt[:, s % 2, h], vw[:, s % 2, h], True, True)
                last.then_inc(su_done, 1)

            pe.wait_ge(q_ready, H)
            pe.wait_ge(cst_ready, 2)
            pe.wait_ge(cols_ready, 2)
            front(0)
            for s in range(NS):
                if s + 1 < NS:
                    front(s + 1)
                back(s)
                if s < MODC - MOD_A:
                    modulation(MOD_A + s)

            for h in range(H):
                pe.wait_ge(hn_ready, NT)
                for n in range(NT):
                    last = pe.transpose(ps[:, 2 * h + n // 4, n % 4 * P:(n % 4 + 1) * P], hs[:, n, h], ident[:])
                last.then_inc(hn_t, 1)
            for r in range(4):
                pe.wait_ge(dg_ready, r + 1)
                if r >= 2:
                    pe.wait_ge(row_c, r - 1)
                for k in range(KT):
                    last = mm(ps[:, 4 + 2 * (r % 2) + k // 4, k % 4 * P:(k % 4 + 1) * P], ones[:],
                              h2T[:, r % 2, k], True, True)
                last.then_inc(row_t, 1)

            def y_tile(k, t):
                src = ygT if k < H else ymT
                return src[:, k % H, t * P:(t + 1) * P]

            pe.wait_ge(ym_ready, 1)
            pw = PIECE["out", 0]
            landed_piece(pe, pw)
            landed_piece(pe, pw + 1)

            def out_projection(t):
                if t >= 2:
                    pe.wait_ge(op_free, t - 1)
                for n in range(2):
                    for k in range(KT):
                        last = mm(ps[:, 2 * (t % 2) + n, :], y_tile(k, t), ring[:, (pw + n) % MSLOT, k, :],
                                  k == 0, k == KT - 1)
                last.then_inc(op_done, 1)

            def to_features(t):
                pe.wait_ge(h2_ready, t + 1)
                pe.wait_ge(row_c, 4)
                if t >= 1:
                    pe.wait_ge(h2_c, t)
                for k in range(KT):
                    last = pe.transpose(ps[:, 4 + k // 4, k % 4 * P:(k % 4 + 1) * P],
                                        h2[:, t % 2, k * P:(k + 1) * P], ident[:])
                last.then_inc(h2_t, 1)

            def route(t):
                pe.wait_ge(h2_c, t + 1)
                if t == 0:
                    pe.wait_ge(wr_in, 16)
                for k in range(KT):
                    last = mm(ps[:, 7, t * NE:(t + 1) * NE], h2T[:, t % 2, k], wr[:, k, :], k == 0, k == KT - 1)
                last.then_inc(rt_done, 1)

            for t in range(NT + 2):
                if t < NT:
                    out_projection(t)
                if t >= 2:
                    to_features(t - 2)
                    route(t - 2)
            pe.wait_ge(aff_ready, 1)
            for n in range(NT):
                last = pe.transpose(ps[0:NE, n // 4, n % 4 * P:(n % 4 + 1) * P], aff[:, n, :], ident[:])
            last.then_inc(aff_t, 1)
            pe.wait_ge(top_ready, 1)
            pe.transpose(ps[:, 2, 0:NE], topf[:], ident[0:NE, 0:NE])
            pe.transpose(ps[:, 2, NE:2 * NE], topv[:], ident[0:NE, 0:NE]).then_inc(top_t, 1)

            def mm3(o, lh, ll, rh, rl, start, stop):
                mm(o, ll, rh, start, False)
                mm(o, lh, rl, False, False)
                return mm(o, lh, rh, False, stop)

            def features(e, r):
                pe.wait_ge(xe_in, e * 16 + 16)
                if isinstance(e, int) and e == 0 and r == 0:
                    pe.wait_ge(idx_ready, 1)
                else:
                    pe.wait_ge(xel_done, 2 * e + r)
                hk = KT // 2
                for k in range(hk):
                    last = pe.transpose(ps[:, 7, k * P:(k + 1) * P], xe[:, (r * hk + k) * P:(r * hk + k + 1) * P],
                                        ident[:])
                last.then_inc(xe_t, 1)

            def expert(e, first, last_one):
                pe.wait_ge(xel_done, 2 * e + 2)
                for m in range(2 * EC):
                    pe.wait_ge(lo_done, e * (2 * EC) + m + 1)
                    pm, hf = m // 2, m % 2
                    if pm < 2 * GUC:
                        q = pm // 2
                        if pm % 2 == 0 and hf == 0 and (not first or q >= 2):
                            pe.wait_ge(hid_done, e * GUC + q - 1)
                        o = ps[:, 2 * (q % 2) + pm % 2, :]
                        for kk in range(KT // 2):
                            k = hf * (KT // 2) + kk
                            last = mm3(o, xeh[:, k], xel[:, k], whv[m % 4][:, kk * W:(kk + 1) * W],
                                       wlv[m % 4][:, kk * W:(kk + 1) * W], k == 0, k == KT - 1)
                    else:
                        if m == 4 * GUC and not first:
                            pe.wait_ge(yw_done, e)
                        if m % 4 == 0 or m >= 4 * GUC + 6:
                            pe.wait_ge(hidl_done, e * GUC + min(GUC, (m - 4 * GUC) // 2 + 1))
                        for kk in range(DK // 2):
                            k = (pm - 2 * GUC) * DK + hf * (DK // 2) + kk
                            for n in range(2):
                                last = mm3(ps[:, 5 + n, :], hidh[:, k], hidl[:, k],
                                           whv[m % 4][:, kk * D + n * W:kk * D + (n + 1) * W],
                                           wlv[m % 4][:, kk * D + n * W:kk * D + (n + 1) * W],
                                           k == 0, k == DE // P - 1)
                    last.then_inc(mm_done, 1)
                    if m % 4 == 1 and 5 <= m < 4 * GUC + 2:
                        q = (m - 5) // 4
                        pe.wait_ge(hid_done, e * GUC + q + 1)
                        if not first or q >= 1:
                            pe.wait_ge(hidl_done, e * GUC + q)
                        for k in range(4):
                            last = pe.transpose(ps[:, 4, k * P:(k + 1) * P], hid[:, q % 2, k * P:(k + 1) * P], ident[:])
                        last.then_inc(hid_t, 1)
                    if not last_one and m in (17, 19):
                        features(e + 1, (m - 17) // 2)

            features(0, 0)
            features(0, 1)
            expert(0, True, False)
            with pe.Fori(1, NE - 1) as e:
                expert(e, False, False)
            expert(NE - 1, False, True)

        @block.vector
        def _(dve):
            link = chain(dve, dve_step)
            dve.wait_ge(vec_t, 1)
            dve.tensor_copy(vcol[:, 0:NVEC], ps[:, 4, 0:NVEC]).then_inc(vcol_ready, 1)
            for t in range(NTC + NT):
                dve.wait_ge(ss_ready, t + 1)
                link(dve.reciprocal(stat[:, 2, t:t + 1], stat[:, 1, t:t + 1]))
                dve.tensor_scalar(xs[:, t % 4, :], xs[:, t % 4, :], stat[:, 2, t:t + 1], None,
                                  ALU.mult).then_inc(xn_ready, 1)

            def bias_cols(a, b):
                bias = vcol[:, VROW["b_mod"] + a:VROW["b_mod"] + b].unsqueeze(2).to_broadcast([P, b - a, 2])
                link(dve.tensor_tensor(mod[:, a:b, :], ps[:, 7, 2 * a:2 * b].rearrange("p (j c) -> p j c", c=2),
                                       bias, ALU.add))

            dve.wait_ge(vcol_ready, 1)
            dve.wait_ge(piece_used, MOD_A)
            bias_cols(0, 2 * KT)
            mixg = vcol[:, VROW["mix_g"]:VROW["mix_g"] + KT].unsqueeze(2).to_broadcast([P, KT, 2])
            link(dve.scalar_tensor_tensor(out=amix[:], in0=mod[:, KT:2 * KT, :], scalar=1.0, in1=mixg,
                                          op0=ALU.add, op1=ALU.mult))
            dve.wait_ge(xt_free, NTC + NT)
            for k in range(KT):
                dve.tensor_scalar(hcT[:, k], hcT[:, k], amix[:, k, 1:2], mod[:, k, 1:2], ALU.mult, ALU.add)
                last = dve.tensor_scalar(hT[:, k], hT[:, k], amix[:, k, 0:1], mod[:, k, 0:1], ALU.mult, ALU.add)
            last.then_inc(h_ready, 1)

            dve.wait_ge(pj_free, 1 + NH2)
            dve.scalar_tensor_tensor(out=rowB[:], in0=rowF[:], scalar=-1.0, in1=rowF[:], op0=ALU.mult,
                                     op1=ALU.min).then_inc(nab_ready, 1)
            dve.wait_ge(lnf_ready, 1)
            link(dve.scalar_tensor_tensor(out=rowF[:], in0=rowF[:], scalar=0.0, in1=rowB[:], op0=ALU.min,
                                          op1=ALU.subtract))
            for d in range(2):
                for j in range(NB):
                    n = block_of(d, j)[1] - block_of(d, j)[0]
                    last = dve.tensor_tensor_scan(run(rowB, d, j), zrow[32 * d:32 * d + H, 0:n], run(rowF, d, j),
                                                  0.0, ALU.add, ALU.add)
            link(last)
            link(dve.tensor_tensor(rowU[:], rowU[:], rowB[:], ALU.subtract))
            dve.nop().then_inc(rowU_ready, 1)
            for j in range(NB):
                for d in range(2):
                    r = slice(32 * d, 32 * d + H)
                    last = dve.tensor_tensor_scan(run(rowM, d, j), run(rowU, d, j), run(rowU, d, j),
                                                  mprev[r, j:j + 1], ALU.max, ALU.max)
                link(last)
                for d in range(2):
                    r = slice(32 * d, 32 * d + H)
                    a, b = block_of(d, j)
                    e0 = b - 1 if d == 0 else a
                    last = dve.tensor_tensor(mprev[r, j + 1:j + 2], rowM[r, e0:e0 + 1], rowB[r, e0:e0 + 1], ALU.add)
                link(last)
            dve.tensor_copy(mprev_t[0:H, 1:NB], mprev[0:H, 1:NB])
            dve.tensor_copy(mprev_t[32:32 + H, 1:NB], mprev[32:32 + H, NB - 1:0:-1])
            dve.tensor_copy(mend_t[0:H, 0:1], rowM[0:H, TC - 1:TC])
            dve.tensor_copy(mend_t[0:H, 1:NB], rowM[0:H, TC + P - 1:TA:P])
            link(dve.tensor_copy(mend_t[32:32 + H, 0:1], rowM[32:32 + H, 0:1]))
            link(dve.tensor_copy(mend_t[32:32 + H, 1:NB], rowM[32:32 + H, TC:TA:P]))

            def lat(t):
                return t[:, TC:TA].rearrange("r (n p) -> r n p", p=P)

            def per_block(t):
                return t[:, 1:NB].unsqueeze(2).to_broadcast([ROWS, NT, P])

            dve.tensor_tensor(decay[:], mprev_t[:], mend_t[:], ALU.subtract)
            dve.tensor_tensor(lat(rowF), per_block(mprev_t), lat(rowM), ALU.subtract)
            link(dve.tensor_tensor(rowB[:, TC:TA], rowB[:, TC:TA], rowM[:, TC:TA], ALU.add))
            dve.tensor_scalar(rowM[:, TC:TA], rowM[:, TC:TA], -1.0, None, ALU.mult).then_inc(rowx_ready, 1)

            def conv(dst, src, n, g0, ct):
                def tap(j):
                    return vcol[:, g0 + j * H + ct:g0 + j * H + ct + 1]
                link(dve.tensor_scalar(dst, src[:, 0:n], tap(0), None, ALU.mult))
                link(dve.scalar_tensor_tensor(out=dst, in0=src[:, 1:n + 1], scalar=tap(1), in1=dst,
                                              op0=ALU.mult, op1=ALU.add))
                return dve.scalar_tensor_tensor(out=dst, in0=src[:, 2:n + 2], scalar=tap(2), in1=dst,
                                                op0=ALU.mult, op1=ALU.add)

            for ct in range(H):
                dve.wait_ge(pj_free, GAT["k", ct, NH2 - 1] + 1)
                link(conv(kTc[:, ct], rawc, TC, VROW["conv_k"], ct))
                conv(kT[:, ct], raw, T, VROW["conv_k"], ct).then_inc(convk_done, 1)
            dve.wait_ge(colU_t, 1)
            dve.tensor_copy(colU[:], ps[:, 4, 0:NT * ROWS].rearrange("p (n r) -> p n r", n=NT)).then_inc(colU_ready, 1)
            dve.tensor_tensor(rowU[:, 0:TC], rowU[:, 0:TC], mend_t[:, 0:1].to_broadcast([ROWS, TC]), ALU.subtract)
            dve.tensor_tensor(lat(rowU), lat(rowU), per_block(mend_t), ALU.subtract).then_inc(roww_ready, 1)

            for n in range(NT):
                dve.wait_ge(pj_free, GAT["vg", n, 0] + 1)
                link(dve.bn_stats(bns[:, n, 0, :], vg[:, n, :]))
                last = dve.bn_aggr(mvg[:, n, :], bns[:, n, 0, :])
            last.then_inc(vgstat_ready, 1)
            dve.wait_ge(vgroot_ready, 1)
            link(dve.reciprocal(rsd[:, :, 0], rsd[:, :, 0]))
            for n in range(NT):
                last = dve.tensor_scalar(vg[:, n, :], vg[:, n, :], mvg[:, n, 0:1], rsd[:, n, 0:1],
                                         ALU.subtract, ALU.mult)
            last.then_inc(vln_ready, 1)
            dve.wait_ge(bs_in, 16)
            dve.wait_ge(pj_free, GAT["u", H - 1, NH2 - 1] + 1)
            for n in range(NT):
                dve.wait_ge(s_done, n + 1)
                tmp = raw[:, 1 + n % 2 * W:1 + (n % 2 + 1) * W].rearrange("p (h t) -> p h t", h=H)
                link(dve.tensor_tensor(tmp, ps[:, 6 + n % 2, :].rearrange("p (h t) -> p h t", h=H), bsb[:], ALU.add))
                yv = ygT[:, :, n * P:(n + 1) * P]
                dve.tensor_tensor(yv, yv, tmp, ALU.mult).then_inc(s_free, 1)
            dve.wait_ge(cols_t, 1)
            dve.tensor_copy(colE[:], ps[:, 4, 0:NT * ROWS].rearrange("p (n r) -> p n r", n=NT))
            dve.tensor_copy(colW[:], ps[:, 5, 0:(NTC + NT) * ROWS].rearrange("p (n r) -> p n r", r=ROWS))\
               .then_inc(cols_ready, 1)
            for ct in range(H):
                dve.wait_ge(pj_free, GAT["q", ct, NH2 - 1] + 1)
                conv(qT[:, ct], raw, T, VROW["conv_q"], ct).then_inc(convq_done, 1)
            dve.wait_ge(cols_t, 2)
            dve.tensor_copy(decb[:], ps[:, 7, 0:2 * H * NB].rearrange("p (r n) -> p r n", r=2 * H)).then_inc(cols_ready, 1)
            dve.wait_ge(cols_ready, 2)

            def weigh(dst, n, d):
                w = colW[:, n, 32 * d:32 * d + H].unsqueeze(2).to_broadcast([P, H, V1])
                return dve.tensor_tensor(dst, vt[:, n], w, ALU.mult)

            for d in range(2):
                if d:
                    dve.wait_ge(cst_done, 1)
                for n in range(NTC):
                    last = weigh(vw[:, n], n, d)
                last.then_inc(cvw_done, 1)
                if d:
                    dve.wait_ge(cst_done, 2)
                else:
                    dve.wait_ge(cst_done, 1)
                for b in range(2):
                    last = dve.tensor_copy(state[:, d, 2 * b:2 * b + 2],
                                           ps[:, CTXBANKS[d][b], 0:2 * V1].rearrange("p (a v) -> p a v", v=V1))
                last.then_inc(cst_ready, 1)
            dve.wait_ge(cst_ready, 2)

            def close_step(s):
                d, c0 = STEPS[s][1], chunk(s)
                j = STEPS[s][0]
                dve.wait_ge(abs_done, s + 1)
                dn = den[:, s % 2]
                link(dve.tensor_tensor(dn[:, 1, :], dn[:, 0, :], colE[:, c0, 32 * d:32 * d + H], ALU.max))
                link(dve.reciprocal(dn[:, 2, :], dn[:, 1, :]))
                for h in range(H):
                    num = ps[:, 4 + h // 2, h % 2 * V1:h % 2 * V1 + P]
                    if j < NT // 2:
                        last = dve.tensor_scalar(hs[:, c0, h], num, dn[:, 2, h:h + 1], None, ALU.mult)
                    else:
                        last = dve.scalar_tensor_tensor(out=hs[:, c0, h], in0=num, scalar=dn[:, 2, h:h + 1],
                                                        in1=hs[:, c0, h], op0=ALU.mult, op1=ALU.add)
                if j < NT // 2:
                    last.then_inc(h_done, 1)
                else:
                    link(last)
                    dve.nop().then_inc(h_done, 1)
                if s < NSU:
                    dve.wait_ge(su_done, s + 1)
                    for h in range(H):
                        upd = ps[:, (6, 0)[h // 2], h % 2 * V1:(h % 2 + 1) * V1]
                        last = dve.scalar_tensor_tensor(out=state[:, d, h], in0=state[:, d, h],
                                                        scalar=decb[:, H * d + h, 1 + c0:2 + c0], in1=upd,
                                                        op0=ALU.mult, op1=ALU.add)
                    last.then_inc(state_up, 1)
                if j >= NT // 2:
                    for h in range(H):
                        last = dve.bn_stats(bns[:, c0, h, :], hs[:, c0, h])
                    link(last)
                    for h in range(H):
                        last = dve.bn_aggr(mv[:, c0, h, :], bns[:, c0, h, :])
                    link(last)

            for s in range(NS + 1):
                if s < NS:
                    d, c0 = STEPS[s][1], chunk(s)
                    if s < NSU:
                        if s >= 2:
                            dve.wait_ge(su_done, s - 1)
                        weigh(vw[:, s % 2], NTC + c0, d).then_inc(vw_done, 1)
                    dve.wait_ge(qk_done, s + 1)
                    if s >= 2:
                        dve.wait_ge(num_done, s - 1)
                    if s >= 4:
                        dve.wait_ge(state_up, min(s - 3, NSU))
                    dve.tensor_tensor(qs[:, s % 2], qT[:, :, c0 * P:(c0 + 1) * P],
                                      ps[:, 3, :].rearrange("p (h t) -> p h t", h=H), ALU.mult).then_inc(qs_done, 1)
                    dve.wait_ge(e_done, s + 1)
                    dve.tensor_tensor(st[:, s % 2], et[:, s % 2],
                                      ps[:, 1, :].rearrange("p (h t) -> p h t", h=H), ALU.mult).then_inc(st_done, 1)
                if s >= 1:
                    if s >= 3:
                        dve.wait_ge(state_up, min(s - 2, NSU))
                    close_step(s - 1)
            dve.nop().then_inc(hstat_ready, 1)
            dve.wait_ge(piece_used, MODC)
            bias_cols(2 * KT, 6 * KT)
            link(dve.scalar_tensor_tensor(out=affn[:], in0=mod[:, 4 * KT:5 * KT, 0], scalar=1.0,
                                          in1=vcol[:, VROW["ffn_g"]:VROW["ffn_g"] + KT], op0=ALU.add, op1=ALU.mult))
            dve.wait_ge(hroot_ready, 1)
            link(dve.reciprocal(rsd[:], rsd[:]))
            for n in range(NT):
                for h in range(H):
                    last = dve.tensor_scalar(hs[:, n, h], hs[:, n, h], mv[:, n, h, 0:1], rsd[:, n, h:h + 1],
                                             ALU.subtract, ALU.mult)
                last.then_inc(hn_ready, 1)
            for h in range(H):
                dve.wait_ge(hn_t, h + 1)
                last = dve.scalar_tensor_tensor(out=ymT[:, h], in0=two(2 * h, 2 * h + 2),
                                                scalar=vcol[:, VROW["mlstm_g"] + h:VROW["mlstm_g"] + h + 1],
                                                in1=ymT[:, h], op0=ALU.mult, op1=ALU.mult)
            last.then_inc(ym_ready, 1)
            dve.wait_ge(ym_ready, 1)
            for r, col in enumerate((lambda k: mod[:, 2 * KT + k, 0:1], lambda k: affn[:, k:k + 1],
                                     lambda k: mod[:, 3 * KT + k, 0:1], lambda k: mod[:, 5 * KT + k, 0:1])):
                if r >= 2:
                    dve.wait_ge(row_t, r - 1)
                for k in range(KT):
                    last = dve.tensor_scalar(h2T[:, r % 2, k], ident[:], col(k), None, ALU.mult)
                last.then_inc(dg_ready, 1)

            def normed(t):
                dve.wait_ge(ss2_ready, t + 1)
                link(dve.reciprocal(stat[:, 2, t:t + 1], stat[:, 1, t:t + 1]))
                if t >= 2:
                    dve.wait_ge(h2_out[t % 2], 16 * (t // 2))
                    dve.wait_ge(h2_t, t - 1)
                link(dve.scalar_tensor_tensor(out=h2[:, t % 2], in0=x2[:, t % 2], scalar=stat[:, 2, t:t + 1],
                                              in1=a2row[:], op0=ALU.mult, op1=ALU.mult))
                dve.tensor_tensor(h2[:, t % 2], h2[:, t % 2], b2row[:], ALU.add).then_inc(h2_ready, 1)

            dve.wait_ge(row_c, 4)
            for t in range(NT):
                dve.wait_ge(op_done, t + 1)
                if t >= 2:
                    dve.wait_ge(x2_out[t % 2], 16 * (t // 2))
                dve.tensor_tensor(x2[:, t % 2], two(2 * (t % 2), 2 * (t % 2) + 2), grow[:], ALU.mult).then_inc(op_free, 1)
                dve.wait_ge(xr_in[t % 2], 16 * (t // 2 + 1))
                dve.wait_ge(op_free, t + 1)
                dve.tensor_tensor(x2[:, t % 2], x2[:, t % 2], xr[:, t % 2], ALU.add).then_inc(x2_ready, 1)
                if t >= 1:
                    normed(t - 1)
            normed(NT - 1)

            dve.wait_ge(rt_done, NT)
            lg = ps[:, 7, 0:NT * NE].rearrange("p (n e) -> p n e", n=NT)
            link(dve.tensor_reduce(srt[:, 0, :], lg, AX.X, ALU.max))
            dve.tensor_tensor(aff[:], lg, srt[:, 0, :].unsqueeze(2).to_broadcast([P, NT, NE]),
                              ALU.subtract).then_inc(ex_arg, 1)
            dve.wait_ge(ex_done, 1)
            link(dve.tensor_reduce(srt[:, 1, :], aff[:], AX.X, ALU.add))
            link(dve.reciprocal(srt[:, 1, :], srt[:, 1, :]))
            dve.tensor_tensor(aff[:], aff[:], srt[:, 1, :].unsqueeze(2).to_broadcast([P, NT, NE]),
                              ALU.mult).then_inc(aff_ready, 1)
            dve.wait_ge(aff_t, 1)
            link(dve.tensor_copy(affT[:], ps[0:NE, 0:2, :].rearrange("p b n -> p (b n)")))
            for r in range(CAP // 8):
                c8 = slice(8 * r, 8 * r + 8)
                link(dve.max(topv[:, c8], affT[:]))
                dve.max_index(topi[:, c8], topv[:, c8], affT[:])
                if r < CAP // 8 - 1:
                    link(dve.match_replace(affT[:], topv[:, c8], affT[:], -1.0))
            link(dve.drain())
            dve.tensor_copy(topf[:], topi[:]).then_inc(top_ready, 1)
            dve.wait_ge(top_t, 1)
            dve.tensor_copy(idx_u[:], ps[:, 2, 0:NE])
            link(dve.tensor_copy(gatec[:], ps[:, 2, NE:2 * NE]))
            dve.nop().then_inc(idx_ready, 1)

            def gather_index(e):
                dve.tensor_copy(idx_e[:, 0:1], idx_u[:, bass.ds(e, 1)]).then_inc(idxg_ready, 1)

            def features_low(e, r):
                hk = KT // 2
                dve.wait_ge(xeh_done, 2 * e + r + 1)
                dve.tensor_tensor(xel[:, r * hk:(r + 1) * hk], ps[:, 7, :].rearrange("p (k t) -> p k t", k=hk),
                                  xeh[:, r * hk:(r + 1) * hk].bitcast(F32), ALU.subtract).then_inc(xel_done, 1)

            def weighted(e, loop):
                if loop:
                    dve.wait_ge(added, 16 * (e + 0))
                dve.tensor_copy(idx_e[:, 1:2], idx_u[:, bass.ds(e, 1)])
                link2(dve.tensor_copy(gate_e[:, 0:1], gatec[:, bass.ds(e, 1)]), e)
                dve.wait_ge(mm_done, e * (2 * EC) + 2 * EC)
                dve.scalar_tensor_tensor(out=yw[:], in0=two(5, 7), scalar=gate_e[:, 0:1], in1=g2row[:],
                                         op0=ALU.mult, op1=ALU.mult).then_inc(yw_done, 1)

            def link2(ins, e):
                ins.then_inc(gate_ready, 1)
                dve.wait_ge(gate_ready, e + 1)

            def expert(e, first, last_one, second=False):
                for m in range(2 * EC):
                    dve.wait_ge(hi_done, e * (2 * EC) + m + 1)
                    dve.tensor_tensor(wlv[m % 4], eview(m), whv[m % 4].bitcast(F32), ALU.subtract).then_inc(lo_done, 1)
                    if m == 3 and not first:
                        weighted(e - 1, not second)
                    if m == 5 and not last_one:
                        dve.wait_ge(xe_in, e * 16 + 16)
                        gather_index(e + 1)
                    if m % 4 == 3 and 7 <= m < 4 * GUC + 4:
                        q = (m - 7) // 4
                        dve.wait_ge(sil_done, e * GUC + q + 1)
                        if not first or q >= 2:
                            dve.wait_ge(hid_t, e * GUC + q - 1)
                        dve.tensor_tensor(hid[:, q % 2], ps[:, 2 * (q % 2) + 1, :], sil[:, q % 2],
                                          ALU.mult).then_inc(hid_done, 1)
                    if m % 4 == 1 and 9 <= m < 4 * GUC + 6:
                        q = (m - 9) // 4
                        dve.wait_ge(hidh_done, e * GUC + q + 1)
                        dve.tensor_tensor(hidl[:, 4 * q:4 * q + 4], ps[:, 4, :].rearrange("p (k t) -> p k t", k=4),
                                          hidh[:, 4 * q:4 * q + 4].bitcast(F32), ALU.subtract).then_inc(hidl_done, 1)
                    if not last_one and m in (21, 23):
                        features_low(e + 1, (m - 21) // 2)

            dve.wait_ge(idx_ready, 1)
            dve.tensor_copy(idx_e[:, 0:1], idx_u[:, 0:1]).then_inc(idxg_ready, 1)
            features_low(0, 0)
            features_low(0, 1)
            expert(0, True, False)
            expert(1, False, False, True)
            with dve.Fori(2, NE - 1) as e:
                expert(e, False, False)
            expert(NE - 1, False, True)
            weighted(NE - 1, True)

            dve.wait_ge(fg_in, 16)
            for t in range(NT):
                dve.wait_ge(froot_ready, t + 1)
                link(dve.reciprocal(stat[:, 2, t:t + 1], stat[:, 1, t:t + 1]))
                dve.scalar_tensor_tensor(out=finv[:, t, :], in0=finv[:, t, :], scalar=stat[:, 2, t:t + 1],
                                         in1=fgrow[:], op0=ALU.mult, op1=ALU.mult).then_inc(fin_ready, 1)


_INS = ['x', 'c', 'ctx', 'c_ctx', 'w_mod', 'b_mod', 'norm_mix_g', 'w_in', 'conv_q', 'conv_k', 'b_igate', 'b_fgate',
        'gmlp_ws', 'gmlp_bs', 'mlstm_norm_g', 'w_out', 'norm_ffn_g', 'w_router', 'w_gate_e', 'w_up_e', 'w_down_e',
        'final_g']


def kernel(**inputs):
    import numpy as np
    from concourse import bacc
    from concourse.bass_utils import run_bass_kernel_spmd

    nc = bacc.Bacc("TRN2", target_bir_lowering=False, num_devices=1)
    arrays, args = {}, []
    for name in _INS:
        a = np.ascontiguousarray(inputs[name])
        arrays[f"in_{name}"] = a
        args.append(nc.dram_tensor(f"in_{name}", a.shape, mybir.dt.from_np(a.dtype), kind="ExternalInput").ap())
    shape = inputs["x"].shape
    out = nc.dram_tensor("out_0", shape, F32, kind="ExternalOutput").ap()
    ffn_in = nc.dram_tensor("ffn_in", shape[1:], F32, kind="Internal").ap()
    stream = nc.dram_tensor("stream", shape[1:], F32, kind="Internal").ap()
    hybrid_block(nc, *args, out, ffn_in, stream)
    r = run_bass_kernel_spmd(nc, [arrays], core_ids=[0])
    return r.results[0]["out_0"]
```

```python
import math
from contextlib import ExitStack

import concourse.bass as bass
from concourse import mybir

ALU = mybir.AluOpType
ACT = mybir.ActivationFunctionType
AX = mybir.AxisListType
F32 = mybir.dt.float32
F32R = mybir.dt.float32r
BF16 = mybir.dt.bfloat16
U32 = mybir.dt.uint32

P = 128
EPS = 1e-6
MASKED = -1e30


def hybrid_block(nc, x, c, ctx, c_ctx, w_mod, b_mod, norm_mix_g, w_in, conv_q, conv_k, b_igate, b_fgate,
                 gmlp_ws, gmlp_bs, mlstm_norm_g, w_out, norm_ffn_g, w_router, w_gate_e, w_up_e,
                 w_down_e, final_g, out, ffn_in, stream, modrows):
    D = x.shape[2]
    T = x.shape[1]
    TC = ctx.shape[1]
    KT = D // P
    NT = T // P
    NTC = TC // P
    NE = w_router.shape[2]
    CAP = 2 * T // NE
    H = gmlp_ws.shape[1]
    W = H * P
    DE = w_gate_e.shape[3]
    ROWS = 32 + H
    TA = TC + T
    NB = NT + 1
    V1 = P + 1
    LOG_INV_SCALE = 0.5 * math.log(P)
    assert CAP == P and W == 512 and D == 1024 and H == 4

    xf = x[0]
    cf = ctx[0]
    win = w_in[0].rearrange("(k p) n -> p k n", p=P)
    wmod = w_mod[0].rearrange("(k p) n -> p k n", p=P)
    wout = w_out[0].rearrange("(k p) n -> p k n", p=P)
    Q0, O0, K0 = 2 * W, 3 * W, 4 * W
    V0, G0 = K0 + W, K0 + 2 * W

    MODC = 6 * D // W
    MOD_A = 2 * D // W
    MOD_B = MODC - MOD_A
    MSLOT = 2
    MOD_ORDER = [0, 2, 1, 3]
    PIECES = [(("mod", i), n % 2) for n, i in enumerate(MOD_ORDER)]
    PIECES += [(("in", K0), 0), (("in", V0), 1)]
    PIECES += [(("mod", MOD_A + i), 0) for i in range(4)] + [(("in", W), 0)]
    PIECES += [(("mod", MOD_A + i), 1) for i in (4, 5)] + [(("in", 0), 1)]
    PIECES += [(("mod", MOD_A + i), 0) for i in (6, 7)] + [(("in", Q0), 0), (("in", O0), 1)]
    PIECES += [(("out", 0), 0), (("out", 1), 1)]
    SLOT = dict(PIECES)
    TURN = {p: sum(s == q for _, q in PIECES[:n + 1]) for n, (p, s) in enumerate(PIECES)}
    ESLOT = 4
    GUC = DE // W
    DK = KT * W // D
    DC = DE // P // DK
    EC = 2 * GUC + DC
    assert EC % ESLOT == 0 and MOD_A == 4 and MOD_B == 8

    es = ExitStack()
    with es:
        def sb(st, name, shape, dt=F32):
            return st.enter_context(nc.sbuf_tensor(name, shape, dt))

        def sem(name):
            return es.enter_context(nc.semaphore(name))

        ring = sb(es, "ring", [P, MSLOT, KT, W])
        ident = sb(es, "ident", [P, P])
        ones = sb(es, "ones", [P, P])
        epsc = sb(es, "epsc", [P, 1])
        vcol = sb(es, "vcol", [P, P])
        scol = sb(es, "scol", [P, KT, 2])
        mod = sb(es, "mod", [P, 2 * KT, 2])
        amix = sb(es, "amix", [P, KT, 2])
        stat = sb(es, "stat", [P, 4, 16])
        g2row = sb(es, "g2row", [P, D])
        idx_f = sb(es, "idx_f", [P, NE])
        idx_u = sb(es, "idx_u", [P, NE], U32)
        gatec = sb(es, "gatec", [P, NE])

        mx = ExitStack()
        ygT = sb(mx, "ygT", [P, H, T])
        hcT = ygT[:, :, :].rearrange("p h t -> p (h t)")[:, 0:KT * TC].rearrange("p (k t) -> p k t", k=KT)
        ymT = sb(mx, "ymT", [P, H, T])
        xs = ymT[:, :, :].rearrange("p h t -> p (h t)").rearrange("p (s d) -> p s d", s=4)
        macc = ymT[:, :, :].rearrange("p h t -> p (h t)").rearrange("p (i n) -> p i n", i=MOD_B)
        m2 = ExitStack()
        identb = sb(m2, "identb", [P, P], BF16)
        maskb = sb(m2, "maskb", [P, 2, H, P], BF16)
        zrow = sb(m2, "zrow", [ROWS, TC])
        rowU = sb(m2, "rowU", [ROWS, TA])
        rowF = sb(m2, "rowF", [ROWS, TA])
        rowB = sb(m2, "rowB", [ROWS, TA])
        rowM = sb(m2, "rowM", [ROWS, TA])
        mprev = sb(m2, "mprev", [ROWS, NB + 1])
        mprev_t = sb(m2, "mprev_t", [ROWS, NB])
        mend_t = sb(m2, "mend_t", [ROWS, NB])
        decay = sb(m2, "decay", [ROWS, NB])
        decb = sb(m2, "decb", [P, 2 * H, NB])
        colU = sb(m2, "colU", [P, NT, ROWS])
        colE = sb(m2, "colE", [P, NT, ROWS])
        colW = sb(m2, "colW", [P, NB + 1, ROWS])
        bns = sb(m2, "bns", [P, NT, H, 6])
        mv = sb(m2, "mv", [P, NT, H, 2])
        mvg = sb(m2, "mvg", [P, NT, 2])
        rsd = sb(m2, "rsd", [P, NT, H])
        floorc = sb(m2, "floorc", [ROWS, 1])
        kT = sb(m2, "kT", [P, H, T])
        kTc = sb(m2, "kTc", [P, H, TC])
        vt = sb(m2, "vt", [P, NTC + NT, H, V1])
        qv = sb(m2, "qv", [P, H * T])
        qT = qv[:, :].rearrange("p (h t) -> p h t", h=H)
        vg = qv[:, :].rearrange("p (n w) -> p n w", n=NT)
        wg = sb(m2, "wg", [P, KT, P])
        sel = wg[:, 0:2 * H]
        pj = ExitStack()
        hT = sb(pj, "hT", [P, KT, T])
        raw = sb(pj, "raw", [P, T + 2])
        rawc = sb(pj, "rawc", [P, TC + 2])
        gbias = sb(pj, "gbias", [P, 1])
        wsT = sb(pj, "wsT", [P, H, P])
        bsb = sb(pj, "bsb", [P, H, P])
        pj.close()
        ml = ExitStack()
        hs = sb(ml, "hs", [P, NT, H, P])
        state = sb(ml, "state", [P, 2, H, V1])
        kt = sb(ml, "kt", [P, 2, H, P])
        et = sb(ml, "et", [P, 2, H, P])
        st = sb(ml, "st", [P, 2, H, P])
        qs = sb(ml, "qs", [P, 2, H, P])
        vw = sb(ml, "vw", [P, 2, H, V1])
        den = sb(ml, "den", [P, 2, 3, H])
        ml.close()
        m2.close()
        op = ExitStack()
        grow = sb(op, "grow", [P, D])
        a2row = sb(op, "a2row", [P, D])
        b2row = sb(op, "b2row", [P, D])
        wr = sb(op, "wr", [P, KT, NE])
        xr = sb(op, "xr", [P, 2, D])
        x2 = sb(op, "x2", [P, 2, D])
        h2 = sb(op, "h2", [P, 2, D])
        h2T = sb(op, "h2T", [P, 2, KT, P])
        sq = sb(op, "sq", [P, D])
        aff = sb(op, "aff", [P, NT // 2, 2, 32])
        eaff = sb(op, "eaff", [P, NT, NE])
        lgT = sb(op, "lgT", [NE, NT, P])
        srt = sb(op, "srt", [P, 2, NT])
        affT = sb(op, "affT", [64, T // 2])
        topv = sb(op, "topv", [64, CAP])
        topi = sb(op, "topi", [64, CAP], U32)
        topf = sb(op, "topf", [64, 2, CAP])
        topc = sb(op, "topc", [P, 2, 2, 32])
        topm = sb(op, "topm", [P, NE])
        op.close()
        mx.close()

        xe = sb(es, "xe", [P, D])
        xeh = sb(es, "xeh", [P, KT, P], F32R)
        xel = sb(es, "xel", [P, KT, P], F32R)
        yw = sb(es, "yw", [P, D])
        wh = sb(es, "wh", [P, 4, KT * W // 2], F32R)
        wl = sb(es, "wl", [P, 4, KT * W // 2], F32R)
        hidh = sb(es, "hidh", [P, DE // P, P], F32R)
        hidl = sb(es, "hidl", [P, DE // P, P], F32R)
        ring2 = sb(es, "ring2", [P, ESLOT - MSLOT, KT, W])
        sil = sb(es, "sil", [P, 2, W])
        hid = sb(es, "hid", [P, 2, W])
        idx_e = sb(es, "idx_e", [P, 2], U32)
        gate_e = sb(es, "gate_e", [P, 2])
        fgrow = sb(es, "fgrow", [P, D])

        ps = es.enter_context(nc.psum_tensor("ps", [P, 8, 512], F32))


        consts_in = sem("consts_in")
        pool_step = sem("pool_step")
        pool_turn = sem("pool_turn")
        act_step = sem("act_step")
        dve_step = sem("dve_step")
        vecs_in = sem("vecs_in")
        ws_in = sem("ws_in")
        bs_in = sem("bs_in")
        gates_in = sem("gates_in")
        x_in = [sem(f"x_in{i}") for i in range(4)]
        piece_in = [sem(f"piece_in{i}") for i in range(MSLOT)]
        moda_done = sem("moda_done")
        moda_c = sem("moda_c")
        moda_t = sem("moda_t")
        moda_ready = sem("moda_ready")
        macc_in = sem("macc_in")
        macc_ready = sem("macc_ready")
        modb_done = sem("modb_done")
        modb_ready = sem("modb_ready")
        modrows_out = sem("modrows_out")
        g_in = sem("g_in")
        s2_in = sem("s2_in")
        g2_in = sem("g2_in")
        a2_ready = sem("a2_ready")
        ss_ready = sem("ss_ready")
        xn_ready = sem("xn_ready")
        xt_ready = sem("xt_ready")
        xt_free = sem("xt_free")
        vec_t = sem("vec_t")
        vcol_ready = sem("vcol_ready")
        scol_ready = sem("scol_ready")
        ws_t = sem("ws_t")
        wsT_ready = sem("wsT_ready")
        h_even = sem("h_even")
        h_odd = sem("h_odd")
        pj_done = sem("pj_done")
        pj_free = sem("pj_free")
        nab_ready = sem("nab_ready")
        lnf_ready = sem("lnf_ready")
        convk_done = sem("convk_done")
        convq_done = sem("convq_done")
        k_ready = sem("k_ready")
        q_ready = sem("q_ready")
        rowU_ready = sem("rowU_ready")
        colU_t = sem("colU_t")
        colU_ready = sem("colU_ready")
        rowx_ready = sem("rowx_ready")
        roww_ready = sem("roww_ready")
        rowe_ready = sem("rowe_ready")
        cols_t = sem("cols_t")
        cols_ready = sem("cols_ready")
        vgstat_ready = sem("vgstat_ready")
        vgroot_ready = sem("vgroot_ready")
        vln_ready = sem("vln_ready")
        s_done = sem("s_done")
        s_free = sem("s_free")
        sel_ready = sem("sel_ready")
        ckt_t = sem("ckt_t")
        ckt_c = sem("ckt_c")
        cvw_done = sem("cvw_done")
        cst_done = sem("cst_done")
        cst_ready = sem("cst_ready")
        kt_t = sem("kt_t")
        kt_c = sem("kt_c")
        m_done = sem("m_done")
        e_done = sem("e_done")
        qk_done = sem("qk_done")
        qs_done = sem("qs_done")
        st_done = sem("st_done")
        vw_done = sem("vw_done")
        num_done = sem("num_done")
        abs_done = sem("abs_done")
        h_done = sem("h_done")
        su_done = sem("su_done")
        state_up = sem("state_up")
        hstat_ready = sem("hstat_ready")
        hroot_ready = sem("hroot_ready")
        hscale_ready = sem("hscale_ready")
        hn_ready = sem("hn_ready")
        hn_t = sem("hn_t")
        ym_ready = sem("ym_ready")
        wr_in = sem("wr_in")
        xr_in = [sem(f"xr_in{i}") for i in range(2)]
        op_done = sem("op_done")
        op_free = sem("op_free")
        x2_ready = sem("x2_ready")
        ss2_ready = sem("ss2_ready")
        h2_ready = sem("h2_ready")
        x2_out = [sem(f"x2_out{i}") for i in range(2)]
        h2_out = [sem(f"h2_out{i}") for i in range(2)]
        h2_t = sem("h2_t")
        h2_c = sem("h2_c")
        rt_done = sem("rt_done")
        lg_c = sem("lg_c")
        lg_t = sem("lg_t")
        ex_arg = sem("ex_arg")
        ex_done = sem("ex_done")
        aff_ready = sem("aff_ready")
        aff_t = sem("aff_t")
        top_ready = sem("top_ready")
        top_t = sem("top_t")
        idx_ready = sem("idx_ready")
        fg_in = sem("fg_in")
        e_in = [sem(f"e_in{i}") for i in range(ESLOT)]
        hi_done = sem("hi_done")
        lo_done = sem("lo_done")
        mm_done = sem("mm_done")
        idxg_ready = sem("idxg_ready")
        xe_in = sem("xe_in")
        xe_t = sem("xe_t")
        xeh_done = sem("xeh_done")
        xel_done = sem("xel_done")
        sil_done = sem("sil_done")
        hid_done = sem("hid_done")
        hid_t = sem("hid_t")
        hidh_done = sem("hidh_done")
        hidl_done = sem("hidl_done")
        yw_done = sem("yw_done")
        added = sem("added")
        gate_ready = sem("gate_ready")
        fin_in = [sem(f"fin_in{i}") for i in range(NT)]
        froot_ready = sem("froot_ready")
        fin_ready = sem("fin_ready")
        out_in = sem("out_in")

        def chain(eng, s):
            n = [0]

            def link(ins):
                n[0] += 1
                ins.then_inc(s, 1)
                eng.wait_ge(s, n[0])
            return link

        def two(a, b):
            return ps[:, a:b, :].rearrange("p b n -> p (b n)")

        whv = [wh[:, i, :] for i in range(4)]
        wlv = [wl[:, i, :] for i in range(4)]
        finv = ring2[:, :, :, :].rearrange("p s k n -> p (s k n)").rearrange("p (t d) -> p t d", t=NT)

        def eview(m):
            i = m // 2 % ESLOT
            v = (ring[:, i] if i < MSLOT else ring2[:, i - MSLOT]).rearrange("p k n -> p (k n)")
            n = KT * W // 2
            return v[:, m % 2 * n:(m % 2 + 1) * n]

        def landed_piece(eng, piece):
            eng.wait_ge(piece_in[SLOT[piece]], 16 * TURN[piece])

        mrow = kT[:, :, 0:W]

        VROW = {}
        at = 0
        for name, n in (("b_mod", 6 * KT), ("c", KT), ("c_ctx", KT), ("mix_g", KT),
                        ("conv_q", 3 * H), ("conv_k", 3 * H), ("mlstm_g", H)):
            VROW[name] = at
            at += n
        NVEC = at
        vecs = g2row[:, 0:P]
        wsraw = g2row[:, P:P + H * P].rearrange("p (h q) -> p h q", h=H)

        HALF = 512
        NH2 = T // HALF
        GROUPS = [("g", 0, 0)] + [("g", 1, h) for h in range(NH2)]
        for ct in range(H):
            GROUPS += [("kc", ct, 0)] + [("k", ct, h) for h in range(NH2)]
        GROUPS += [("vc", n, 0) for n in range(NTC)] + [("v", n, 0) for n in range(NT)]
        GROUPS += [("vg", n, 0) for n in range(NT)]
        for kind in "uqo":
            GROUPS += [(kind, ct, h) for ct in range(H) for h in range(NH2)]
        GAT = {g: n for n, g in enumerate(GROUPS)}
        PIECE_OF = {"kc": ("in", K0), "k": ("in", K0), "vc": ("in", V0), "v": ("in", V0), "vg": ("in", W),
                    "u": ("in", 0), "o": ("in", O0), "q": ("in", Q0)}

        def block_of(d, j):
            if j == 0:
                return 0, TC
            c0 = j - 1 if d == 0 else NT - j
            return TC + c0 * P, TC + (c0 + 1) * P

        def run(t, d, j):
            a, b = block_of(d, j)
            v = t[32 * d:32 * d + H, a:b]
            return v if d == 0 else v[:, ::-1]

        START = "t0 t1 t2 t3 r0 t4 t5 c0 r1 t6 t7 c1 r2 t8 t9 c2 r3 c3".split()
        STEPS = [(j, d) for j in range(NT) for d in range(2)]
        NS = len(STEPS)
        NSU = NS - 2

        def chunk(s):
            j, d = STEPS[s]
            return j if d == 0 else NT - 1 - j

        ORDER = [chunk(s) for s in range(NT, NS)]

        CTXBANKS = ((4, 5), (6, 1))

        block = es.enter_context(nc.Block())

        @block.gpsimd
        def _(pool):
            link = chain(pool, pool_step)
            for t in range(4):
                src = cf[t * P:(t + 1) * P, :] if t < NTC else xf[(t - NTC) * P:(t - NTC + 1) * P, :]
                pool.dma_start(xs[:, t, :], src).then_inc(x_in[t], 16)
            link(pool.memset(ident[:], 0.0))
            link(pool.affine_select(out=ident[:], in_=ident[:], compare_op=ALU.not_equal, fill=1.0, base=0,
                                    pattern=[[-1, P]], channel_multiplier=1))
            pool.memset(ones[:], 1.0)
            pool.memset(epsc[:], EPS)
            pool.tensor_copy(identb[:], ident[:])
            pool.memset(floorc[:], LOG_INV_SCALE)
            pool.memset(zrow[:], 0.0)
            pool.memset(rowB[:], 0.0)
            pool.memset(rowM[:], 0.0)
            pool.memset(mprev[:], 0.0)
            pool.memset(mend_t[:], 0.0)
            pool.memset(mprev_t[:], 0.0)
            pool.memset(raw[:, 0:1], 0.0)
            pool.memset(raw[:, T + 1:T + 2], 0.0)
            pool.memset(rawc[:, 0:1], 0.0)
            pool.memset(rawc[:, TC + 1:TC + 2], 0.0)
            pool.memset(vt[:, :, :, P:V1], 1.0)
            link(pool.memset(gbias[:], 0.0))
            link(pool.memset(wg[:], 0.0))
            link(pool.memset(maskb[:], 0.0))
            for d, sign in ((0, 1), (1, -1)):
                link(pool.affine_select(out=maskb[:, d], in_=maskb[:, d], compare_op=ALU.is_ge, fill=MASKED,
                                        base=0, pattern=[[0, H], [sign, P]], channel_multiplier=-sign))
            pool.sem_inc(consts_in, 1)
            for n in range(4):
                src = w_in[0][:, G0 + H * n:G0 + H * (n + 1)].rearrange("(k p) n -> p k n", p=P)
                pool.dma_start(wg[:, :, 32 * n:32 * n + H], src).then_inc(gates_in, 16)
                b = (b_igate, b_fgate)[n // 2][0, n % 2].rearrange("(h a) -> h a", a=1)
                pool.dma_start(gbias[32 * n:32 * n + H, :], b).then_inc(gates_in, 16)
            pool.dma_start(bsb[:], gmlp_bs[0].partition_broadcast(P)).then_inc(bs_in, 16)
            for t in range(4, NTC + NT):
                pool.wait_ge(xt_ready, t - 3)
                pool.dma_start(xs[:, t % 4, :], xf[(t - NTC) * P:(t - NTC + 1) * P, :]).then_inc(x_in[t % 4], 16)
            pool.wait_ge(pj_done, 1 + NH2)
            link(pool.memset(sel[:], 0.0))
            for d in range(2):
                for h in range(H):
                    last = pool.affine_select(out=sel[:, H * d + h], in_=sel[:, H * d + h],
                                              compare_op=ALU.not_equal, fill=1.0, base=-(32 * d + h),
                                              pattern=[[0, P]], channel_multiplier=1)
            link(last)
            pool.sem_inc(sel_ready, 1)
            pool.wait_ge(xt_ready, NTC + NT)
            link(pool.memset(macc[:], 0.0))
            pool.dma_start(macc[0:1].rearrange("p i n -> p (i n)"),
                           b_mod[0:1, MOD_A * W:MODC * W]).then_inc(macc_in, 16)
            pool.wait_ge(modb_ready, MOD_B)
            pool.dma_start(modrows, macc[0:1].rearrange("p i n -> p (i n)")).then_inc(modrows_out, 16)
            pool.wait_ge(ym_ready, NT)
            pool.dma_start(wr[:], w_router[0].rearrange("(k p) n -> p k n", p=P)).then_inc(wr_in, 16)
            for dst, src, s in ((grow, modrows[:, 0:D], g_in), (b2row, modrows[:, D:2 * D], s2_in),
                                (a2row, modrows[:, 2 * D:3 * D], s2_in), (sq, norm_ffn_g, s2_in),
                                (g2row, modrows[:, 3 * D:4 * D], g2_in)):
                pool.dma_start(dst[:], src[0].partition_broadcast(P)).then_inc(s, 16)
            for t in range(NT):
                if t >= 2:
                    pool.wait_ge(x2_ready, t - 1)
                pool.dma_start(xr[:, t % 2, :], xf[ORDER[t] * P:(ORDER[t] + 1) * P, :]).then_inc(xr_in[t % 2], 16)
            pool.wait_ge(g2_in, 16)
            pool.wait_ge(idx_ready, 1)
            pool.dma_start(fgrow[:], final_g.partition_broadcast(P)).then_inc(fg_in, 16)
            for i in range(2):
                pool.wait_ge(h2_out[i], 16 * (NT // 2))
                pool.wait_ge(x2_out[i], 16 * (NT // 2))

            def gather(e):
                pool.sem_inc(pool_turn, 1)
                pool.indirect_dma_start(
                    out=xe[:, :], out_offset=None, in_=ffn_in,
                    in_offset=bass.IndirectOffsetOnAxis(ap=idx_e[:, 0:1], axis=0)).then_inc(xe_in, 16)

            def scatter(e):
                pool.wait_ge(yw_done, e + 1)
                pool.sem_inc(pool_turn, 1)
                pool.indirect_dma_start(
                    out=stream, out_offset=bass.IndirectOffsetOnAxis(ap=idx_e[:, 1:2], axis=0),
                    in_=yw[:, :], in_offset=None, compute_op=ALU.add).then_inc(added, 16)

            pool.wait_ge(idxg_ready, 1)
            gather(0)
            pool.wait_ge(idxg_ready, 2)
            pool.wait_ge(xe_t, 2)
            gather(1)
            with pool.Fori(1, NE - 1) as e:
                scatter(e - 1)
                pool.wait_ge(idxg_ready, e + 2)
                pool.wait_ge(xe_t, 2 * e + 2)
                gather(e + 1)
                pool.wait_ge(added, 16 * e)
            scatter(NE - 2)
            pool.wait_ge(added, 16 * (NE - 1))
            scatter(NE - 1)
            pool.wait_ge(added, 16 * NE)

        @block.sync
        def _(sp):
            before = {}
            for n, ((kind, c0), slot) in enumerate(PIECES):
                if n < 2:
                    sp.wait_ge(x_in[2 * n + 1], 16)
                if slot in before:
                    k0, i0 = before[slot]
                    if k0 == "mod" and i0 < MOD_A:
                        sp.wait_ge(moda_done, MOD_ORDER.index(i0) + 1)
                    elif k0 == "mod":
                        sp.wait_ge(macc_ready, i0 - MOD_A + 1)
                    else:
                        sp.wait_ge(pj_done, 1 + max(g for g, v in enumerate(GROUPS) if PIECE_OF.get(v[0]) == (k0, i0)))
                src = {"mod": lambda: wmod[:, :, c0 * W:(c0 + 1) * W], "in": lambda: win[:, :, c0:c0 + W],
                       "out": lambda: wout[:, :, c0 * W:(c0 + 1) * W]}[kind]()
                sp.dma_start(ring[:, slot], src).then_inc(piece_in[slot], 16)
                before[slot] = kind, c0

            def eslot(m):
                return ring[:, m] if m < MSLOT else ring2[:, m - MSLOT]

            def load(e, m):
                if m < 2 * GUC:
                    w, c0 = (w_gate_e, w_up_e)[m % 2], m // 2 * W
                    src = w[0][e, :, c0:c0 + W].rearrange("(k p) n -> p k n", p=P)
                    dst = eslot(m % ESLOT)
                else:
                    r0 = (m - 2 * GUC) * DK * P
                    src = w_down_e[0][e, r0:r0 + DK * P, :].rearrange("(k p) n -> p k n", p=P)
                    dst = eslot(m % ESLOT).rearrange("p k n -> p (k n)").rearrange("p (k n) -> p k n", k=DK)
                sp.dma_start(dst, src).then_inc(e_in[m % ESLOT], 16)

            for m in range(EC):
                if m < MSLOT:
                    sp.wait_ge(op_done, NT)
                elif m < ESLOT:
                    sp.wait_ge(ym_ready, NT)
                else:
                    sp.wait_ge(lo_done, 2 * (m - ESLOT + 1))
                load(0, m)
            with sp.Fori(1, NE) as e:
                for m in range(EC):
                    sp.wait_ge(lo_done, e * (2 * EC) + 2 * (m - ESLOT + 1))
                    load(e, m)
            sp.wait_ge(lo_done, 2 * EC * NE)
            sp.wait_ge(added, 16 * NE)
            for t in range(NT):
                sp.dma_start(finv[:, t, :], stream[t * P:(t + 1) * P, :]).then_inc(fin_in[t], 16)
            for t in range(NT):
                sp.wait_ge(fin_ready, t + 1)
                sp.dma_start(out[0][t * P:(t + 1) * P, :], finv[:, t, :]).then_inc(out_in, 16)
            sp.wait_ge(out_in, 16 * NT)

        @block.scalar
        def _(act):
            link = chain(act, act_step)
            rows = {"b_mod": b_mod[0], "c": c[0], "c_ctx": c_ctx, "mix_g": norm_mix_g[0], 
                    "conv_q": conv_q[0].rearrange("j n -> (j n)"), "conv_k": conv_k[0].rearrange("j n -> (j n)"),
                    "mlstm_g": mlstm_norm_g[0]}
            for name, v in rows.items():
                n = v.shape[0] // P
                act.dma_start(vecs[VROW[name]:VROW[name] + n, :], v.rearrange("(r p) -> r p", p=P)).then_inc(vecs_in, 16)
            act.dma_start(wsraw[:], gmlp_ws[0].rearrange("h p q -> p h q")).then_inc(ws_in, 16)
            act.wait_ge(vcol_ready, 1)
            act.activation(scol[:].rearrange("p k c -> p c k"),
                           vcol[:, VROW["c"]:VROW["c"] + 2 * KT].rearrange("p (c k) -> p c k", c=2),
                           ACT.Silu).then_inc(scol_ready, 1)
            act.wait_ge(consts_in, 1)

            def norm_copy(t):
                act.wait_ge(xt_ready, t + 1)
                dst = hcT[:, :, t * P:(t + 1) * P] if t < NTC else hT[:, :, (t - NTC) * P:(t - NTC + 1) * P]
                b = 2 * (t % 2)
                act.activation(dst, two(b, b + 2).rearrange("p (k t) -> p k t", k=KT), ACT.Copy).then_inc(xt_free, 1)

            for t in range(NTC + NT):
                act.wait_ge(x_in[t % 4], 16 * (t // 4 + 1))
                if t >= 1:
                    act.wait_ge(ss_ready, t)
                link(act.activation(raw[:, 1:1 + D], xs[:, t % 4, :], ACT.Square, accum_out=stat[:, 0, t:t + 1]))
                act.activation(stat[:, 1, t:t + 1], stat[:, 0, t:t + 1], ACT.Sqrt, bias=epsc[:],
                               scale=1.0 / D).then_inc(ss_ready, 1)
                if t >= 1:
                    norm_copy(t - 1)
            norm_copy(NTC + NT - 1)
            act.wait_ge(xt_free, NTC + NT)
            for half in range(2):
                act.wait_ge(moda_ready, 2 * half + 2)
                for src, cond in ((hcT, 1), (hT, 0)):
                    for k in range(half * KT // 2 + 1, (half + 1) * KT // 2, 2):
                        act.activation(src[:, k], src[:, k], ACT.Identity, scale=amix[:, k, cond:cond + 1],
                                       bias=mod[:, k, cond:cond + 1]).then_inc(h_odd, 1)
            act.wait_ge(ws_t, 1)
            act.activation(wsT[:], ps[:, 6, :].rearrange("p (h q) -> p h q", h=H), ACT.Copy).then_inc(wsT_ready, 1)

            def take(g, dst, src, f=ACT.Copy):
                act.wait_ge(pj_done, g + 1)
                act.activation(dst, src, f).then_inc(pj_free, 1)

            act.wait_ge(gates_in, 8 * 16)
            for kind, blk, h in GROUPS[0:1 + NH2]:
                g = GAT[kind, blk, h]
                a, n = (0, TC) if blk == 0 else (TC + h * HALF, HALF)
                act.wait_ge(pj_done, g + 1)
                act.activation(rowU[:, a:a + n], ps[0:ROWS, g % 4, 0:n], ACT.Identity, bias=gbias[0:ROWS, :])
                act.activation(rowF[:, a:a + n], ps[64:64 + ROWS, g % 4, 0:n], ACT.Identity,
                               bias=gbias[64:64 + ROWS, :]).then_inc(pj_free, 1)
            act.wait_ge(nab_ready, 1)
            link(act.activation(rowB[:], rowB[:], ACT.Exp))
            act.activation(rowB[:], rowB[:], ACT.Ln, bias=1.0).then_inc(lnf_ready, 1)
            for ct in range(H):
                if ct >= 1:
                    act.wait_ge(convk_done, ct)
                g = GAT["kc", ct, 0]
                take(g, rawc[:, 1:1 + TC], ps[:, g % 4, 0:TC])
                for h in range(NH2):
                    g = GAT["k", ct, h]
                    take(g, raw[:, 1 + h * HALF:1 + (h + 1) * HALF], ps[:, g % 4, :])
                if ct >= 1:
                    act.activation(kTc[:, ct - 1], kTc[:, ct - 1], ACT.Silu)
                    act.activation(kT[:, ct - 1], kT[:, ct - 1], ACT.Silu).then_inc(k_ready, 1)
            act.wait_ge(convk_done, H)
            act.activation(kTc[:, H - 1], kTc[:, H - 1], ACT.Silu)
            act.activation(kT[:, H - 1], kT[:, H - 1], ACT.Silu).then_inc(k_ready, 1)
            for n in range(NTC + NT):
                g = GAT[("vc", n, 0) if n < NTC else ("v", n - NTC, 0)]
                take(g, vt[:, n, :, 0:P], ps[:, g % 4, :].rearrange("p (h d) -> p h d", h=H))
            act.wait_ge(rowx_ready, 1)
            act.activation(decay[:], decay[:], ACT.Exp)
            act.activation(rowF[:, TC:TA], rowF[:, TC:TA], ACT.Exp)
            act.activation(rowB[:, TC:TA], rowB[:, TC:TA], ACT.Exp, scale=-1.0, bias=floorc[:]).then_inc(rowe_ready, 1)
            act.wait_ge(roww_ready, 1)
            act.activation(rowU[:], rowU[:], ACT.Exp).then_inc(rowe_ready, 1)
            for n in range(NT):
                g = GAT["vg", n, 0]
                take(g, vg[:, n, :], ps[:, g % 4, :], ACT.Gelu_apprx_tanh)
            for ct in range(H):
                for h in range(NH2):
                    g = GAT["u", ct, h]
                    take(g, ygT[:, ct, h * HALF:(h + 1) * HALF], ps[:, g % 4, :], ACT.Gelu_apprx_tanh)
                if ct == 0:
                    act.wait_ge(vgstat_ready, 1)
                    act.activation(rsd[:, :, 0], mvg[:, :, 1], ACT.Sqrt, bias=epsc[:]).then_inc(vgroot_ready, 1)
            act.wait_ge(s_free, NT)
            for ct in range(H):
                if ct >= 1:
                    act.wait_ge(convq_done, ct)
                for h in range(NH2):
                    g = GAT["q", ct, h]
                    take(g, raw[:, 1 + h * HALF:1 + (h + 1) * HALF], ps[:, g % 4, :])
                if ct >= 1:
                    act.activation(qT[:, ct - 1], qT[:, ct - 1], ACT.Silu).then_inc(q_ready, 1)
            act.wait_ge(convq_done, H)
            act.activation(qT[:, H - 1], qT[:, H - 1], ACT.Silu).then_inc(q_ready, 1)
            act.wait_ge(modrows_out, 16)
            for ct in range(H):
                for h in range(NH2):
                    g = GAT["o", ct, h]
                    act.wait_ge(pj_done, g + 1)
                    half_o = ymT[:, ct, h * HALF:(h + 1) * HALF]
                    link(act.activation(half_o, ps[:, g % 4, :], ACT.Sigmoid))
                    act.activation(half_o, half_o, ACT.Copy,
                                   scale=vcol[:, VROW["mlstm_g"] + ct:VROW["mlstm_g"] + ct + 1]).then_inc(pj_free, 1)

            for n in range(NTC):
                act.wait_ge(ckt_t, n + 1)
                act.activation(kt[:, n], ps[:, 2 * n, :].rearrange("p (h d) -> p h d", h=H), ACT.Copy).then_inc(ckt_c, 1)
            act.wait_ge(colU_ready, 1)
            for s in range(NS + 4):
                if s < NS:
                    d, c0 = STEPS[s][1], chunk(s)
                    act.wait_ge(m_done, s + 1)
                    if s >= 2:
                        act.wait_ge(st_done, s - 1)
                    for h in range(H):
                        last = act.activation(et[:, s % 2, h], ps[:, 2, h * P:(h + 1) * P], ACT.Exp,
                                              bias=colU[:, c0, 32 * d + h:32 * d + h + 1])
                    last.then_inc(e_done, 1)
                    if s < NSU:
                        act.wait_ge(kt_t, s + 1)
                        act.wait_ge(cst_done, 2)
                        if s >= 2:
                            act.wait_ge(su_done, s - 1)
                        act.activation(kt[:, s % 2], ps[:, 0, :].rearrange("p (h d) -> p h d", h=H),
                                       ACT.Copy).then_inc(kt_c, 1)
                if 1 <= s <= NS:
                    act.wait_ge(num_done, s)
                    if s >= 3:
                        act.wait_ge(h_done, s - 2)
                    act.activation(den[:, (s - 1) % 2, 0, :].rearrange("p (a b) -> p a b", a=2),
                                   ps[:, 4:6, 0:2 * V1].rearrange("p a (b v) -> p a b v", v=V1)[:, :, :, P],
                                   ACT.Abs).then_inc(abs_done, 1)
                if NT <= s - 3 < NS:
                    n = s - 3 - NT
                    c1 = chunk(s - 3)
                    act.wait_ge(hscale_ready, n + 1)
                    for h in range(H):
                        last = act.activation(hs[:, c1, h], hs[:, c1, h], ACT.Identity, scale=rsd[:, c1, h:h + 1],
                                              bias=mv[:, c1, h, 0:1])
                    last.then_inc(hn_ready, 1)
                if NT <= s - 2 < NS:
                    n = s - 2 - NT
                    c1 = chunk(s - 2)
                    act.wait_ge(hstat_ready, n + 1)
                    act.activation(rsd[:, c1], mv[:, c1, :, 1], ACT.Sqrt, bias=epsc[:]).then_inc(hroot_ready, 1)

            def feature_copy(t):
                act.wait_ge(h2_t, t + 1)
                if t >= 2:
                    act.wait_ge(rt_done, t - 1)
                act.activation(h2T[:, t % 2], two(4, 6).rearrange("p (k t) -> p k t", k=KT),
                               ACT.Copy).then_inc(h2_c, 1)

            def logit_copy(t):
                act.wait_ge(rt_done, t + 1)
                act.activation(lgT[:, ORDER[t], :], ps[0:NE, 7, 0:P], ACT.Copy).then_inc(lg_c, 1)

            for t in range(NT):
                act.wait_ge(x2_ready, t + 1)
                act.dma_start(stream[ORDER[t] * P:(ORDER[t] + 1) * P, :], x2[:, t % 2, :]).then_inc(x2_out[t % 2], 16)
                if t >= 1:
                    act.wait_ge(ss2_ready, t)
                else:
                    act.wait_ge(a2_ready, 1)
                link(act.activation(sq[:], x2[:, t % 2, :], ACT.Square, accum_out=stat[:, 0, t:t + 1]))
                act.activation(stat[:, 1, t:t + 1], stat[:, 0, t:t + 1], ACT.Sqrt, bias=epsc[:],
                               scale=1.0 / D).then_inc(ss2_ready, 1)
                if t >= 1:
                    act.wait_ge(h2_ready, t)
                    act.dma_start(ffn_in[ORDER[t - 1] * P:(ORDER[t - 1] + 1) * P, :], h2[:, (t - 1) % 2, :]).then_inc(h2_out[(t - 1) % 2], 16)
                    feature_copy(t - 1)
                if t >= 2:
                    logit_copy(t - 2)
            act.wait_ge(h2_ready, NT)
            act.dma_start(ffn_in[ORDER[NT - 1] * P:(ORDER[NT - 1] + 1) * P, :], h2[:, (NT - 1) % 2, :]).then_inc(h2_out[(NT - 1) % 2], 16)
            logit_copy(NT - 2)
            feature_copy(NT - 1)
            logit_copy(NT - 1)
            act.wait_ge(ex_arg, 1)
            act.activation(eaff[:], eaff[:], ACT.Exp).then_inc(ex_done, 1)

            def features_high(e, r):
                act.wait_ge(xe_t, 2 * e + r + 1)
                hk = KT // 2
                act.activation(xeh[:, r * hk:(r + 1) * hk], ps[:, 7, :].rearrange("p (k t) -> p k t", k=hk),
                               ACT.Copy).then_inc(xeh_done, 1)

            def split_high(e, m, first):
                if m % 2 == 0:
                    pm = m // 2
                    act.wait_ge(e_in[pm % ESLOT], e * (16 * EC // ESLOT) + 16 * (pm // ESLOT + 1))
                if not first or m >= 4:
                    act.wait_ge(mm_done, e * (2 * EC) + m - 3)
                act.activation(whv[m % 4], eview(m), ACT.Copy).then_inc(hi_done, 1)

            def expert(e, first, last):
                for m in range(2 * EC):
                    if not first or m >= 4:
                        split_high(e, m, first)
                    if m % 4 == 3 and 7 <= m < 4 * GUC + 4:
                        q = (m - 7) // 4
                        act.wait_ge(mm_done, e * (2 * EC) + 4 * q + 4)
                        if not first or q >= 2:
                            act.wait_ge(hid_done, e * GUC + q - 1)
                        act.activation(sil[:, q % 2], ps[:, 2 * (q % 2), :], ACT.Silu).then_inc(sil_done, 1)
                    if m % 4 == 1 and 9 <= m < 4 * GUC + 6:
                        q = (m - 9) // 4
                        act.wait_ge(hid_t, e * GUC + q + 1)
                        act.activation(hidh[:, 4 * q:4 * q + 4], ps[:, 4, :].rearrange("p (k t) -> p k t", k=4),
                                       ACT.Copy).then_inc(hidh_done, 1)
                    if not last and m in (21, 23):
                        features_high(e + 1, (m - 21) // 2)

            for m in range(4):
                split_high(0, m, True)
            act.wait_ge(idx_ready, 1)
            features_high(0, 0)
            features_high(0, 1)
            expert(0, True, False)
            with act.Fori(1, NE - 1) as e:
                expert(e, False, False)
            expert(NE - 1, False, True)

            for t in range(NT):
                act.wait_ge(fin_in[t], 16)
                if t >= 1:
                    act.wait_ge(froot_ready, t)
                else:
                    act.wait_ge(hid_done, NE * GUC)
                link(act.activation(sil[:].rearrange("p a n -> p (a n)"), finv[:, t, :], ACT.Square,
                                    accum_out=stat[:, 0, t:t + 1]))
                act.activation(stat[:, 1, t:t + 1], stat[:, 0, t:t + 1], ACT.Sqrt, bias=epsc[:],
                               scale=1.0 / D).then_inc(froot_ready, 1)

        @block.tensor
        def _(pe):
            def mm(o, l, r, start, stop):
                return pe.matmul(o, l, r, start=start, stop=stop)

            pe.wait_ge(consts_in, 1)
            pe.wait_ge(vecs_in, 16 * 7)
            pe.transpose(ps[:, 4, 0:NVEC], vecs[0:NVEC, :], ident[0:NVEC, 0:NVEC]).then_inc(vec_t, 1)

            def token_tile(t):
                pe.wait_ge(xn_ready, t + 1)
                if t >= 2:
                    pe.wait_ge(xt_free, t - 1)
                for k in range(KT):
                    last = pe.transpose(ps[:, 2 * (t % 2) + k // 4, k % 4 * P:(k % 4 + 1) * P],
                                        xs[:, t % 4, k * P:(k + 1) * P], ident[:])
                last.then_inc(xt_ready, 1)

            def mod_rows(n):
                piece = "mod", MOD_ORDER[n]
                landed_piece(pe, piece)
                if n == 1:
                    pe.wait_ge(vcol_ready, 1)
                if n >= 2:
                    pe.wait_ge(moda_c, n - 1)
                for k in range(KT):
                    last = mm(ps[0:2, (6, 4)[n % 2], :], scol[:, k, :], ring[:, SLOT[piece], k, :],
                              k == 0, k == KT - 1)
                last.then_inc(moda_done, 1)

            def mod_cols(n):
                pe.wait_ge(moda_c, n + 1)
                if n >= 2:
                    pe.wait_ge(moda_ready, n - 1)
                for ct in range(W // P):
                    last = pe.transpose(ps[:, (7, 5)[n % 2], 2 * ct:2 * ct + 2], mrow[0:2, n, ct * P:(ct + 1) * P],
                                        ident[0:2, 0:2])
                last.then_inc(moda_t, 1)

            for what in START:
                {"t": token_tile, "r": mod_rows, "c": mod_cols}[what[0]](int(what[1:]))
            pe.wait_ge(ws_in, 16)
            for h in range(H):
                last = pe.transpose(ps[:, 6, h * P:(h + 1) * P], wsraw[:, h], ident[:])
            last.then_inc(ws_t, 1)
            pe.wait_ge(gates_in, 8 * 16)
            pe.wait_ge(xt_free, NTC + NT)

            def features_ready(k, c):
                half, n = k // (KT // 2), k % (KT // 2) // 2
                pe.wait_ge((h_even, h_odd)[k % 2], half * KT // 2 + (KT // 4) * c + n + 1)

            def group(g):
                kind, i, h = GROUPS[g]
                if g >= 4:
                    pe.wait_ge(pj_free, g - 3)
                o = ps[:, g % 4, :]
                if kind == "g":
                    src, a, n = (hcT, 0, TC) if i == 0 else (hT, h * HALF, HALF)
                    for k in range(KT):
                        features_ready(k, min(i, 1))
                        last = mm(o[:, 0:n], wg[:, k, :], src[:, k, a:a + n], k == 0, k == KT - 1)
                    last.then_inc(pj_done, 1)
                    return
                piece = PIECE_OF[kind]
                w = ring[:, SLOT[piece]]
                first = GROUPS[g - 1][0] == "g" or PIECE_OF[GROUPS[g - 1][0]] != PIECE_OF[kind]
                if first:
                    landed_piece(pe, piece)
                for k in range(KT):
                    if kind in ("vc", "v", "vg"):
                        src = hcT if kind == "vc" else hT
                        last = mm(o, src[:, k, i * P:(i + 1) * P], w[:, k, :], k == 0, k == KT - 1)
                    elif kind == "kc":
                        last = mm(o[:, 0:TC], w[:, k, i * P:(i + 1) * P], hcT[:, k, :], k == 0, k == KT - 1)
                    else:
                        last = mm(o, w[:, k, i * P:(i + 1) * P], hT[:, k, h * HALF:(h + 1) * HALF],
                                  k == 0, k == KT - 1)
                last.then_inc(pj_done, 1)

            for g in range(GAT["vg", 0, 0]):
                group(g)
            pe.wait_ge(rowU_ready, 1)
            for n in range(NT):
                last = pe.transpose(ps[:, 4, n * ROWS:(n + 1) * ROWS], rowU[:, TC + n * P:TC + (n + 1) * P],
                                    ident[0:ROWS, 0:ROWS])
            last.then_inc(colU_t, 1)
            for g in range(GAT["vg", 0, 0], GAT["q", 0, 0]):
                group(g)
                i = g - GAT["u", 0, 0]
                if 0 <= i < MOD_B:
                    pe.wait_ge(macc_ready, i + 1)
                    if i >= 3:
                        pe.wait_ge(modb_ready, i - 2)
                    mm(ps[0:1, 5 + i % 3, :], ones[:, 0:1], macc[:, i, :], True, True).then_inc(modb_done, 1)
            pe.wait_ge(vln_ready, 1)
            pe.wait_ge(modb_ready, MOD_B)
            pe.wait_ge(wsT_ready, 1)
            for n in range(NT):
                if n >= 2:
                    pe.wait_ge(s_free, n - 1)
                for h in range(H):
                    last = mm(ps[:, 6 + n % 2, h * P:(h + 1) * P], vg[:, n, h * P:(h + 1) * P], wsT[:, h], True, True)
                last.then_inc(s_done, 1)
            pe.wait_ge(rowe_ready, 2)
            pe.wait_ge(colU_ready, 1)
            for n in range(NT):
                pe.transpose(ps[:, 4, n * ROWS:(n + 1) * ROWS], rowB[:, TC + n * P:TC + (n + 1) * P],
                             ident[0:ROWS, 0:ROWS])
            for n in range(NTC + NT):
                last = pe.transpose(ps[:, 5, n * ROWS:(n + 1) * ROWS], rowU[:, n * P:(n + 1) * P],
                                    ident[0:ROWS, 0:ROWS])
            last.then_inc(cols_t, 1)
            for g in range(GAT["q", 0, 0], GAT["o", 0, 0]):
                group(g)
            pe.wait_ge(sel_ready, 1)
            pe.wait_ge(s_free, NT)
            for r in range(2 * H):
                last = mm(ps[:, 7, r * NB:(r + 1) * NB], sel[0:ROWS, r], decay[:], True, True)
            last.then_inc(cols_t, 1)

            for g in range(GAT["o", 0, 0], len(GROUPS)):
                group(g)

            pe.wait_ge(k_ready, H)
            pe.wait_ge(cols_ready, 1)
            pe.wait_ge(pj_free, len(GROUPS))
            for n in range(NTC):
                for h in range(H):
                    last = pe.transpose(ps[:, 2 * n, h * P:(h + 1) * P], kTc[:, h, n * P:(n + 1) * P], ident[:])
                last.then_inc(ckt_t, 1)
            pe.wait_ge(ckt_c, NTC)
            for d in range(2):
                pe.wait_ge(cvw_done, d + 1)
                for h in range(H):
                    o = ps[:, CTXBANKS[d][h // 2], h % 2 * V1:(h % 2 + 1) * V1]
                    for n in range(NTC):
                        last = mm(o, kt[:, n, h], vw[:, n, h], n == 0, n == NTC - 1)
                last.then_inc(cst_done, 1)

            def front(s):
                d, c0 = STEPS[s][1], chunk(s)
                a, b = c0 * P, (c0 + 1) * P
                if s >= 1:
                    pe.wait_ge(e_done, s)
                mm(ps[:, 2, :], identb[:], maskb[:, d].rearrange("p h t -> p (h t)"), True, False)
                for h in range(H):
                    last = mm(ps[:, 2, h * P:(h + 1) * P], sel[0:ROWS, H * d + h], rowM[:, TC + a:TC + b],
                              False, h == H - 1)
                last.then_inc(m_done, 1)
                if s >= 1:
                    pe.wait_ge(qs_done, s)
                    pe.wait_ge(st_done, s)
                for h in range(H):
                    mm(ps[:, 3, h * P:(h + 1) * P], sel[0:ROWS, H * d + h], rowF[:, TC + a:TC + b], True, True)
                for h in range(H):
                    last = mm(ps[:, 1, h * P:(h + 1) * P], kT[:, h, a:b], qT[:, h, a:b], True, True)
                last.then_inc(qk_done, 1)
                if s < NSU:
                    if s >= 2:
                        pe.wait_ge(state_up, s - 1)
                    if s >= 1:
                        pe.wait_ge(kt_c, s)
                    for h in range(H):
                        last = pe.transpose(ps[:, 0, h * P:(h + 1) * P], kT[:, h, a:b], ident[:])
                    last.then_inc(kt_t, 1)

            def back(s):
                d, c0 = STEPS[s][1], chunk(s)
                pe.wait_ge(st_done, s + 1)
                pe.wait_ge(qs_done, s + 1)
                if s >= 2:
                    pe.wait_ge(state_up, s - 1)
                if s >= 1:
                    pe.wait_ge(h_done, s)
                for h in range(H):
                    o = ps[:, 4 + h // 2, h % 2 * V1:(h % 2 + 1) * V1]
                    mm(o, st[:, s % 2, h], vt[:, NTC + c0, h], True, False)
                    last = mm(o, qs[:, s % 2, h], state[:, d, h], False, True)
                last.then_inc(num_done, 1)
                if s >= NSU:
                    return
                pe.wait_ge(kt_c, min(s + 2, NSU))
                pe.wait_ge(vw_done, s + 1)
                if s >= 1:
                    pe.wait_ge(state_up, s)
                for h in range(H):
                    o = ps[:, (6, 0)[h // 2], h % 2 * V1:(h % 2 + 1) * V1]
                    last = mm(o, kt[:, s % 2, h], vw[:, s % 2, h], True, True)
                last.then_inc(su_done, 1)

            pe.wait_ge(q_ready, H)
            pe.wait_ge(cst_ready, 2)
            pe.wait_ge(cols_ready, 2)
            front(0)
            for s in range(NS + 3):
                if s + 1 < NS:
                    front(s + 1)
                if s < NS:
                    back(s)
                if NT <= s - 3:
                    n = s - 3 - NT
                    pe.wait_ge(hn_ready, n + 1)
                    if n >= 1:
                        pe.wait_ge(ym_ready, n)
                    for h in range(H):
                        last = pe.transpose(ps[:, 7, h * P:(h + 1) * P], hs[:, chunk(s - 3), h], ident[:])
                    last.then_inc(hn_t, 1)

            def y_tile(k, t):
                src = ygT if k < H else ymT
                return src[:, k % H, t * P:(t + 1) * P]

            landed_piece(pe, ("out", 0))
            landed_piece(pe, ("out", 1))

            def out_projection(t):
                pe.wait_ge(ym_ready, t + 1)
                if t < 2:
                    pe.wait_ge(h_done, NS)
                    pe.wait_ge(state_up, NSU)
                else:
                    pe.wait_ge(op_free, t - 1)
                for n in range(2):
                    for k in range(KT):
                        last = mm(ps[:, 2 * (t % 2) + n, :], y_tile(k, ORDER[t]), ring[:, SLOT["out", n], k, :],
                                  k == 0, k == KT - 1)
                last.then_inc(op_done, 1)

            def to_features(t):
                pe.wait_ge(h2_ready, t + 1)
                if t >= 1:
                    pe.wait_ge(h2_c, t)
                for k in range(KT):
                    last = pe.transpose(ps[:, 4 + k // 4, k % 4 * P:(k % 4 + 1) * P],
                                        h2[:, t % 2, k * P:(k + 1) * P], ident[:])
                last.then_inc(h2_t, 1)

            def route(t):
                pe.wait_ge(h2_c, t + 1)
                if t == 0:
                    pe.wait_ge(wr_in, 16)
                    pe.wait_ge(ym_ready, NT)
                if t >= 1:
                    pe.wait_ge(lg_c, t)
                for k in range(KT):
                    last = mm(ps[0:NE, 7, 0:P], wr[:, k, :], h2T[:, t % 2, k], k == 0, k == KT - 1)
                last.then_inc(rt_done, 1)

            for t in range(NT + 2):
                if t < NT:
                    out_projection(t)
                if t >= 2:
                    to_features(t - 2)
                    route(t - 2)
            pe.wait_ge(lg_c, NT)
            for n in range(NT):
                last = pe.transpose(ps[:, 6, n * NE:(n + 1) * NE], lgT[:, n, :], ident[0:NE, 0:NE])
            last.then_inc(lg_t, 1)
            pe.wait_ge(aff_ready, 1)
            for n in range(NT // 2):
                last = pe.transpose(ps[0:64, 0, n * P:(n + 1) * P], aff[:, n].rearrange("p a e -> p (a e)"), ident[:])
            last.then_inc(aff_t, 1)
            pe.wait_ge(top_ready, 1)
            for i in range(2):
                last = pe.transpose(ps[:, 2, 64 * i:64 * (i + 1)], topf[:, i], ident[0:64, 0:64])
            last.then_inc(top_t, 1)

            def mm3(o, lh, ll, rh, rl, start, stop):
                mm(o, ll, rh, start, False)
                mm(o, lh, rl, False, False)
                return mm(o, lh, rh, False, stop)

            def features(e, r):
                pe.wait_ge(xe_in, e * 16 + 16)
                if isinstance(e, int) and e == 0 and r == 0:
                    pe.wait_ge(idx_ready, 1)
                else:
                    pe.wait_ge(xel_done, 2 * e + r)
                hk = KT // 2
                for k in range(hk):
                    last = pe.transpose(ps[:, 7, k * P:(k + 1) * P], xe[:, (r * hk + k) * P:(r * hk + k + 1) * P],
                                        ident[:])
                last.then_inc(xe_t, 1)

            def expert(e, first, last_one):
                pe.wait_ge(xel_done, 2 * e + 2)
                for m in range(2 * EC):
                    pe.wait_ge(lo_done, e * (2 * EC) + m + 1)
                    pm, hf = m // 2, m % 2
                    if pm < 2 * GUC:
                        q = pm // 2
                        if pm % 2 == 0 and hf == 0 and (not first or q >= 2):
                            pe.wait_ge(hid_done, e * GUC + q - 1)
                        o = ps[:, 2 * (q % 2) + pm % 2, :]
                        for kk in range(KT // 2):
                            k = hf * (KT // 2) + kk
                            last = mm3(o, xeh[:, k], xel[:, k], whv[m % 4][:, kk * W:(kk + 1) * W],
                                       wlv[m % 4][:, kk * W:(kk + 1) * W], k == 0, k == KT - 1)
                    else:
                        if m == 4 * GUC and not first:
                            pe.wait_ge(yw_done, e)
                        if m % 4 == 0 or m >= 4 * GUC + 6:
                            pe.wait_ge(hidl_done, e * GUC + min(GUC, (m - 4 * GUC) // 2 + 1))
                        for kk in range(DK // 2):
                            k = (pm - 2 * GUC) * DK + hf * (DK // 2) + kk
                            for n in range(2):
                                last = mm3(ps[:, 5 + n, :], hidh[:, k], hidl[:, k],
                                           whv[m % 4][:, kk * D + n * W:kk * D + (n + 1) * W],
                                           wlv[m % 4][:, kk * D + n * W:kk * D + (n + 1) * W],
                                           k == 0, k == DE // P - 1)
                    last.then_inc(mm_done, 1)
                    if m % 4 == 1 and 5 <= m < 4 * GUC + 2:
                        q = (m - 5) // 4
                        pe.wait_ge(hid_done, e * GUC + q + 1)
                        if not first or q >= 1:
                            pe.wait_ge(hidl_done, e * GUC + q)
                        for k in range(4):
                            last = pe.transpose(ps[:, 4, k * P:(k + 1) * P], hid[:, q % 2, k * P:(k + 1) * P], ident[:])
                        last.then_inc(hid_t, 1)
                    if not last_one and m in (17, 19):
                        features(e + 1, (m - 17) // 2)

            features(0, 0)
            features(0, 1)
            expert(0, True, False)
            with pe.Fori(1, NE - 1) as e:
                expert(e, False, False)
            expert(NE - 1, False, True)

        @block.vector
        def _(dve):
            link = chain(dve, dve_step)
            dve.wait_ge(vec_t, 1)
            dve.tensor_copy(vcol[:, 0:NVEC], ps[:, 4, 0:NVEC]).then_inc(vcol_ready, 1)

            def token_norm(t):
                dve.wait_ge(ss_ready, t + 1)
                link(dve.reciprocal(stat[:, 2, t:t + 1], stat[:, 1, t:t + 1]))
                dve.tensor_scalar(xs[:, t % 4, :], xs[:, t % 4, :], stat[:, 2, t:t + 1], None,
                                  ALU.mult).then_inc(xn_ready, 1)

            def mod_copy(n):
                dve.wait_ge(moda_done, n + 1)
                dve.tensor_copy(mrow[0:2, n, :], ps[0:2, (6, 4)[n % 2], :]).then_inc(moda_c, 1)

            def mod_bias(n):
                nc4 = W // P
                a = MOD_ORDER[n] * nc4
                bias = vcol[:, VROW["b_mod"] + a:VROW["b_mod"] + a + nc4].unsqueeze(2).to_broadcast([P, nc4, 2])
                dve.wait_ge(moda_t, n + 1)
                link(dve.tensor_tensor(mod[:, a:a + nc4, :],
                                       ps[:, (7, 5)[n % 2], 0:2 * nc4].rearrange("p (j c) -> p j c", c=2),
                                       bias, ALU.add))
                if a >= KT:
                    k = a - KT
                    mixg = vcol[:, VROW["mix_g"] + k:VROW["mix_g"] + k + nc4].unsqueeze(2).to_broadcast([P, nc4, 2])
                    link(dve.scalar_tensor_tensor(out=amix[:, k:k + nc4], in0=mod[:, a:a + nc4, :], scalar=1.0,
                                                  in1=mixg, op0=ALU.add, op1=ALU.mult))
                dve.nop().then_inc(moda_ready, 1)

            for what in START:
                if what[0] == "t":
                    token_norm(int(what[1:]))
                elif what[0] == "r":
                    mod_copy(int(what[1:]))
                else:
                    mod_bias(int(what[1:]))
            dve.wait_ge(xt_free, NTC + NT)
            for half in range(2):
                dve.wait_ge(moda_ready, 2 * half + 2)
                for src, cond in ((hcT, 1), (hT, 0)):
                    for k in range(half * KT // 2, (half + 1) * KT // 2, 2):
                        dve.tensor_scalar(src[:, k], src[:, k], amix[:, k, cond:cond + 1], mod[:, k, cond:cond + 1],
                                          ALU.mult, ALU.add).then_inc(h_even, 1)

            def mod_partial(i):
                piece = "mod", MOD_A + i
                landed_piece(dve, piece)
                for k in range(KT):
                    link(dve.scalar_tensor_tensor(out=macc[:, i, :], in0=ring[:, SLOT[piece], k, :],
                                                  scalar=scol[:, k, 0:1], in1=macc[:, i, :],
                                                  op0=ALU.mult, op1=ALU.add))
                dve.nop().then_inc(macc_ready, 1)

            dve.wait_ge(pj_free, 1 + NH2)
            dve.scalar_tensor_tensor(out=rowB[:], in0=rowF[:], scalar=-1.0, in1=rowF[:], op0=ALU.mult,
                                     op1=ALU.min).then_inc(nab_ready, 1)
            dve.wait_ge(lnf_ready, 1)
            link(dve.scalar_tensor_tensor(out=rowF[:], in0=rowF[:], scalar=0.0, in1=rowB[:], op0=ALU.min,
                                          op1=ALU.subtract))
            for d in range(2):
                for j in range(NB):
                    n = block_of(d, j)[1] - block_of(d, j)[0]
                    last = dve.tensor_tensor_scan(run(rowB, d, j), zrow[32 * d:32 * d + H, 0:n], run(rowF, d, j),
                                                  0.0, ALU.add, ALU.add)
            link(last)
            link(dve.tensor_tensor(rowU[:], rowU[:], rowB[:], ALU.subtract))
            dve.nop().then_inc(rowU_ready, 1)
            for j in range(NB):
                for d in range(2):
                    r = slice(32 * d, 32 * d + H)
                    last = dve.tensor_tensor_scan(run(rowM, d, j), run(rowU, d, j), run(rowU, d, j),
                                                  mprev[r, j:j + 1], ALU.max, ALU.max)
                link(last)
                for d in range(2):
                    r = slice(32 * d, 32 * d + H)
                    a, b = block_of(d, j)
                    e0 = b - 1 if d == 0 else a
                    last = dve.tensor_tensor(mprev[r, j + 1:j + 2], rowM[r, e0:e0 + 1], rowB[r, e0:e0 + 1], ALU.add)
                link(last)
            dve.tensor_copy(mprev_t[0:H, 1:NB], mprev[0:H, 1:NB])
            dve.tensor_copy(mprev_t[32:32 + H, 1:NB], mprev[32:32 + H, NB - 1:0:-1])
            dve.tensor_copy(mend_t[0:H, 0:1], rowM[0:H, TC - 1:TC])
            dve.tensor_copy(mend_t[0:H, 1:NB], rowM[0:H, TC + P - 1:TA:P])
            link(dve.tensor_copy(mend_t[32:32 + H, 0:1], rowM[32:32 + H, 0:1]))
            link(dve.tensor_copy(mend_t[32:32 + H, 1:NB], rowM[32:32 + H, TC:TA:P]))

            def lat(t):
                return t[:, TC:TA].rearrange("r (n p) -> r n p", p=P)

            def per_block(t):
                return t[:, 1:NB].unsqueeze(2).to_broadcast([ROWS, NT, P])

            dve.tensor_tensor(decay[:], mprev_t[:], mend_t[:], ALU.subtract)
            dve.tensor_tensor(lat(rowF), per_block(mprev_t), lat(rowM), ALU.subtract)
            link(dve.tensor_tensor(rowB[:, TC:TA], rowB[:, TC:TA], rowM[:, TC:TA], ALU.add))
            dve.tensor_scalar(rowM[:, TC:TA], rowM[:, TC:TA], -1.0, None, ALU.mult).then_inc(rowx_ready, 1)

            def conv(dst, src, n, g0, ct):
                def tap(j):
                    return vcol[:, g0 + j * H + ct:g0 + j * H + ct + 1]
                link(dve.tensor_scalar(dst, src[:, 0:n], tap(0), None, ALU.mult))
                link(dve.scalar_tensor_tensor(out=dst, in0=src[:, 1:n + 1], scalar=tap(1), in1=dst,
                                              op0=ALU.mult, op1=ALU.add))
                return dve.scalar_tensor_tensor(out=dst, in0=src[:, 2:n + 2], scalar=tap(2), in1=dst,
                                                op0=ALU.mult, op1=ALU.add)

            for ct in range(H):
                dve.wait_ge(pj_free, GAT["k", ct, NH2 - 1] + 1)
                link(conv(kTc[:, ct], rawc, TC, VROW["conv_k"], ct))
                conv(kT[:, ct], raw, T, VROW["conv_k"], ct).then_inc(convk_done, 1)
            dve.wait_ge(macc_in, 16)
            for i in range(4):
                mod_partial(i)
            dve.wait_ge(colU_t, 1)
            dve.tensor_copy(colU[:], ps[:, 4, 0:NT * ROWS].rearrange("p (n r) -> p n r", n=NT)).then_inc(colU_ready, 1)
            dve.tensor_tensor(rowU[:, 0:TC], rowU[:, 0:TC], mend_t[:, 0:1].to_broadcast([ROWS, TC]), ALU.subtract)
            dve.tensor_tensor(lat(rowU), lat(rowU), per_block(mend_t), ALU.subtract).then_inc(roww_ready, 1)


            for n in range(NT):
                if n == 2:
                    for i in (4, 5):
                        mod_partial(i)
                dve.wait_ge(pj_free, GAT["vg", n, 0] + 1)
                link(dve.bn_stats(bns[:, n, 0, :], vg[:, n, :]))
                last = dve.bn_aggr(mvg[:, n, :], bns[:, n, 0, :])
            last.then_inc(vgstat_ready, 1)
            for i in (6, 7):
                mod_partial(i)
            dve.wait_ge(vgroot_ready, 1)
            link(dve.reciprocal(rsd[:, :, 0], rsd[:, :, 0]))
            for n in range(NT):
                last = dve.tensor_scalar(vg[:, n, :], vg[:, n, :], mvg[:, n, 0:1], rsd[:, n, 0:1],
                                         ALU.subtract, ALU.mult)
            last.then_inc(vln_ready, 1)
            for i in range(MOD_B):
                dve.wait_ge(modb_done, i + 1)
                last = dve.tensor_copy(macc[0:1, i, :], ps[0:1, 5 + i % 3, :]).then_inc(modb_ready, 1)
            dve.wait_ge(bs_in, 16)
            dve.wait_ge(pj_free, GAT["u", H - 1, NH2 - 1] + 1)
            for n in range(NT):
                dve.wait_ge(s_done, n + 1)
                tmp = raw[:, 1 + n % 2 * W:1 + (n % 2 + 1) * W].rearrange("p (h t) -> p h t", h=H)
                link(dve.tensor_tensor(tmp, ps[:, 6 + n % 2, :].rearrange("p (h t) -> p h t", h=H), bsb[:], ALU.add))
                yv = ygT[:, :, n * P:(n + 1) * P]
                dve.tensor_tensor(yv, yv, tmp, ALU.mult).then_inc(s_free, 1)
            dve.wait_ge(cols_t, 1)
            dve.tensor_copy(colE[:], ps[:, 4, 0:NT * ROWS].rearrange("p (n r) -> p n r", n=NT))
            dve.tensor_copy(colW[:], ps[:, 5, 0:(NTC + NT) * ROWS].rearrange("p (n r) -> p n r", r=ROWS))\
               .then_inc(cols_ready, 1)
            for ct in range(H):
                dve.wait_ge(pj_free, GAT["q", ct, NH2 - 1] + 1)
                conv(qT[:, ct], raw, T, VROW["conv_q"], ct).then_inc(convq_done, 1)
            dve.wait_ge(cols_t, 2)
            dve.tensor_copy(decb[:], ps[:, 7, 0:2 * H * NB].rearrange("p (r n) -> p r n", r=2 * H)).then_inc(cols_ready, 1)
            dve.wait_ge(cols_ready, 2)

            def weigh(dst, n, d):
                w = colW[:, n, 32 * d:32 * d + H].unsqueeze(2).to_broadcast([P, H, V1])
                return dve.tensor_tensor(dst, vt[:, n], w, ALU.mult)

            for d in range(2):
                if d:
                    dve.wait_ge(cst_done, 1)
                for n in range(NTC):
                    last = weigh(vw[:, n], n, d)
                last.then_inc(cvw_done, 1)
                if d:
                    dve.wait_ge(cst_done, 2)
                else:
                    dve.wait_ge(cst_done, 1)
                for b in range(2):
                    last = dve.tensor_copy(state[:, d, 2 * b:2 * b + 2],
                                           ps[:, CTXBANKS[d][b], 0:2 * V1].rearrange("p (a v) -> p a v", v=V1))
                last.then_inc(cst_ready, 1)
            dve.wait_ge(cst_ready, 2)

            def close_step(s):
                d, c0 = STEPS[s][1], chunk(s)
                j = STEPS[s][0]
                dve.wait_ge(abs_done, s + 1)
                dn = den[:, s % 2]
                link(dve.tensor_tensor(dn[:, 1, :], dn[:, 0, :], colE[:, c0, 32 * d:32 * d + H], ALU.max))
                link(dve.reciprocal(dn[:, 2, :], dn[:, 1, :]))
                for h in range(H):
                    num = ps[:, 4 + h // 2, h % 2 * V1:h % 2 * V1 + P]
                    if j < NT // 2:
                        last = dve.tensor_scalar(hs[:, c0, h], num, dn[:, 2, h:h + 1], None, ALU.mult)
                    else:
                        last = dve.scalar_tensor_tensor(out=hs[:, c0, h], in0=num, scalar=dn[:, 2, h:h + 1],
                                                        in1=hs[:, c0, h], op0=ALU.mult, op1=ALU.add)
                if j < NT // 2:
                    last.then_inc(h_done, 1)
                else:
                    link(last)
                    dve.nop().then_inc(h_done, 1)
                if s < NSU:
                    dve.wait_ge(su_done, s + 1)
                    for h in range(H):
                        upd = ps[:, (6, 0)[h // 2], h % 2 * V1:(h % 2 + 1) * V1]
                        last = dve.scalar_tensor_tensor(out=state[:, d, h], in0=state[:, d, h],
                                                        scalar=decb[:, H * d + h, 1 + c0:2 + c0], in1=upd,
                                                        op0=ALU.mult, op1=ALU.add)
                    last.then_inc(state_up, 1)
                if j >= NT // 2:
                    for h in range(H):
                        last = dve.bn_stats(bns[:, c0, h, :], hs[:, c0, h])
                    link(last)
                    for h in range(H):
                        last = dve.bn_aggr(mv[:, c0, h, :], bns[:, c0, h, :])
                    last.then_inc(hstat_ready, 1)

            for s in range(NS + 4):
                if s < NS:
                    d, c0 = STEPS[s][1], chunk(s)
                    if s < NSU:
                        if s >= 2:
                            dve.wait_ge(su_done, s - 1)
                        weigh(vw[:, s % 2], NTC + c0, d).then_inc(vw_done, 1)
                    dve.wait_ge(qk_done, s + 1)
                    if s >= 2:
                        dve.wait_ge(num_done, s - 1)
                    if s >= 4:
                        dve.wait_ge(state_up, min(s - 3, NSU))
                    dve.tensor_tensor(qs[:, s % 2], qT[:, :, c0 * P:(c0 + 1) * P],
                                      ps[:, 3, :].rearrange("p (h t) -> p h t", h=H), ALU.mult).then_inc(qs_done, 1)
                    dve.wait_ge(e_done, s + 1)
                    dve.tensor_tensor(st[:, s % 2], et[:, s % 2],
                                      ps[:, 1, :].rearrange("p (h t) -> p h t", h=H), ALU.mult).then_inc(st_done, 1)
                if 1 <= s <= NS:
                    if s >= 3:
                        dve.wait_ge(state_up, min(s - 2, NSU))
                    close_step(s - 1)
                if NT <= s - 2 < NS:
                    n, c1 = s - 2 - NT, chunk(s - 2)
                    dve.wait_ge(hroot_ready, n + 1)
                    link(dve.reciprocal(rsd[:, c1], rsd[:, c1]))
                    dve.scalar_tensor_tensor(out=mv[:, c1, :, 0], in0=mv[:, c1, :, 0], scalar=-1.0, in1=rsd[:, c1],
                                             op0=ALU.mult, op1=ALU.mult).then_inc(hscale_ready, 1)
                if NT <= s - 4 < NS:
                    n, c1 = s - 4 - NT, chunk(s - 4)
                    dve.wait_ge(hn_t, n + 1)
                    yv = ymT[:, :, c1 * P:(c1 + 1) * P]
                    dve.tensor_tensor(yv, yv, ps[:, 7, :].rearrange("p (h t) -> p h t", h=H),
                                      ALU.mult).then_inc(ym_ready, 1)

            def normed(t):
                dve.wait_ge(ss2_ready, t + 1)
                link(dve.reciprocal(stat[:, 2, t:t + 1], stat[:, 1, t:t + 1]))
                if t >= 2:
                    dve.wait_ge(h2_out[t % 2], 16 * (t // 2))
                    dve.wait_ge(h2_t, t - 1)
                link(dve.scalar_tensor_tensor(out=h2[:, t % 2], in0=x2[:, t % 2], scalar=stat[:, 2, t:t + 1],
                                              in1=a2row[:], op0=ALU.mult, op1=ALU.mult))
                dve.tensor_tensor(h2[:, t % 2], h2[:, t % 2], b2row[:], ALU.add).then_inc(h2_ready, 1)

            dve.wait_ge(s2_in, 3 * 16)
            dve.scalar_tensor_tensor(out=a2row[:], in0=a2row[:], scalar=1.0, in1=sq[:], op0=ALU.add,
                                     op1=ALU.mult).then_inc(a2_ready, 1)
            dve.wait_ge(a2_ready, 1)
            dve.wait_ge(g_in, 16)
            for t in range(NT):
                dve.wait_ge(op_done, t + 1)
                if t >= 2:
                    dve.wait_ge(x2_out[t % 2], 16 * (t // 2))
                dve.tensor_tensor(x2[:, t % 2], two(2 * (t % 2), 2 * (t % 2) + 2), grow[:], ALU.mult).then_inc(op_free, 1)
                dve.wait_ge(xr_in[t % 2], 16 * (t // 2 + 1))
                dve.wait_ge(op_free, t + 1)
                dve.tensor_tensor(x2[:, t % 2], x2[:, t % 2], xr[:, t % 2], ALU.add).then_inc(x2_ready, 1)
                if t >= 1:
                    normed(t - 1)
            normed(NT - 1)

            dve.wait_ge(lg_t, 1)
            lg = ps[:, 6, 0:NT * NE].rearrange("p (n e) -> p n e", n=NT)
            link(dve.memset(aff[:], 0.0))
            link(dve.tensor_reduce(srt[:, 0, :], lg, AX.X, ALU.max))
            dve.tensor_tensor(eaff[:], lg, srt[:, 0, :].unsqueeze(2).to_broadcast([P, NT, NE]),
                              ALU.subtract).then_inc(ex_arg, 1)
            dve.wait_ge(ex_done, 1)
            link(dve.tensor_reduce(srt[:, 1, :], eaff[:], AX.X, ALU.add))
            link(dve.reciprocal(srt[:, 1, :], srt[:, 1, :]))
            for q in range(2):
                n = slice(q * NT // 2, (q + 1) * NT // 2)
                last = dve.tensor_tensor(aff[:, :, q, 0:NE], eaff[:, n],
                                         srt[:, 1, n].unsqueeze(2).to_broadcast([P, NT // 2, NE]), ALU.mult)
            last.then_inc(aff_ready, 1)
            dve.wait_ge(aff_t, 1)
            link(dve.tensor_copy(affT[:], ps[0:64, 0, :]))
            for r in range(CAP // 8):
                c8 = slice(8 * r, 8 * r + 8)
                link(dve.max(topv[:, c8], affT[:]))
                dve.max_index(topi[:, c8], topv[:, c8], affT[:])
                if r < CAP // 8 - 1:
                    link(dve.match_replace(affT[:], topv[:, c8], affT[:], -1.0))
            link(dve.drain())
            dve.tensor_copy(topf[0:32, 0], topi[0:32])
            dve.tensor_copy(topf[0:32, 1], topv[0:32])
            dve.tensor_copy(topf[32:64, 1], topv[32:64, ::-1])
            link(dve.tensor_copy(topf[32:64, 0], topi[32:64, ::-1]))
            link(dve.tensor_scalar(topf[32:64, 0], topf[32:64, 0], float(T // 2), None, ALU.add))
            dve.nop().then_inc(top_ready, 1)
            dve.wait_ge(top_t, 1)
            link(dve.tensor_copy(topc[:].rearrange("p i a e -> p (i a e)"), ps[:, 2, 0:P]))
            ia, ib, va, vb = (topc[:, i, q, 0:NE] for i in range(2) for q in range(2))
            dve.tensor_tensor(gatec[:], va, vb, ALU.max)
            dve.tensor_tensor(topm[:], va, vb, ALU.is_ge)
            link(dve.tensor_tensor(idx_f[:], ia, ib, ALU.subtract))
            link(dve.tensor_tensor(idx_f[:], idx_f[:], topm[:], ALU.mult))
            link(dve.tensor_tensor(idx_u[:], idx_f[:], ib, ALU.add))
            dve.nop().then_inc(idx_ready, 1)

            def gather_index(e):
                dve.tensor_copy(idx_e[:, 0:1], idx_u[:, bass.ds(e, 1)]).then_inc(idxg_ready, 1)

            def features_low(e, r):
                hk = KT // 2
                dve.wait_ge(xeh_done, 2 * e + r + 1)
                dve.tensor_tensor(xel[:, r * hk:(r + 1) * hk], ps[:, 7, :].rearrange("p (k t) -> p k t", k=hk),
                                  xeh[:, r * hk:(r + 1) * hk].bitcast(F32), ALU.subtract).then_inc(xel_done, 1)

            def weighted(e, loop):
                if loop:
                    dve.wait_ge(added, 16 * (e + 0))
                dve.tensor_copy(idx_e[:, 1:2], idx_u[:, bass.ds(e, 1)])
                link2(dve.tensor_copy(gate_e[:, 0:1], gatec[:, bass.ds(e, 1)]), e)
                dve.wait_ge(mm_done, e * (2 * EC) + 2 * EC)
                dve.scalar_tensor_tensor(out=yw[:], in0=two(5, 7), scalar=gate_e[:, 0:1], in1=g2row[:],
                                         op0=ALU.mult, op1=ALU.mult).then_inc(yw_done, 1)

            def link2(ins, e):
                ins.then_inc(gate_ready, 1)
                dve.wait_ge(gate_ready, e + 1)

            def split_low(e, m):
                dve.wait_ge(hi_done, e * (2 * EC) + m + 1)
                dve.tensor_tensor(wlv[m % 4], eview(m), whv[m % 4].bitcast(F32), ALU.subtract).then_inc(lo_done, 1)

            def expert(e, first, last_one, second=False):
                for m in range(2 * EC):
                    if not first or m >= 2:
                        split_low(e, m)
                    if m == 3 and not first:
                        weighted(e - 1, not second)
                    if m == 5 and not last_one:
                        dve.wait_ge(xe_in, e * 16 + 16)
                        gather_index(e + 1)
                    if m % 4 == 3 and 7 <= m < 4 * GUC + 4:
                        q = (m - 7) // 4
                        dve.wait_ge(sil_done, e * GUC + q + 1)
                        if not first or q >= 2:
                            dve.wait_ge(hid_t, e * GUC + q - 1)
                        dve.tensor_tensor(hid[:, q % 2], ps[:, 2 * (q % 2) + 1, :], sil[:, q % 2],
                                          ALU.mult).then_inc(hid_done, 1)
                    if m % 4 == 1 and 9 <= m < 4 * GUC + 6:
                        q = (m - 9) // 4
                        dve.wait_ge(hidh_done, e * GUC + q + 1)
                        dve.tensor_tensor(hidl[:, 4 * q:4 * q + 4], ps[:, 4, :].rearrange("p (k t) -> p k t", k=4),
                                          hidh[:, 4 * q:4 * q + 4].bitcast(F32), ALU.subtract).then_inc(hidl_done, 1)
                    if not last_one and m in (21, 23):
                        features_low(e + 1, (m - 21) // 2)

            dve.wait_ge(idx_ready, 1)
            dve.tensor_copy(idx_e[:, 0:1], idx_u[:, 0:1]).then_inc(idxg_ready, 1)
            for i in range(2):
                dve.wait_ge(x2_out[i], 16 * (NT // 2))
                dve.wait_ge(h2_out[i], 16 * (NT // 2))
            for m in range(2):
                split_low(0, m)
            features_low(0, 0)
            features_low(0, 1)
            expert(0, True, False)
            expert(1, False, False, True)
            with dve.Fori(2, NE - 1) as e:
                expert(e, False, False)
            expert(NE - 1, False, True)
            weighted(NE - 1, True)

            dve.wait_ge(fg_in, 16)
            for t in range(NT):
                dve.wait_ge(froot_ready, t + 1)
                link(dve.reciprocal(stat[:, 2, t:t + 1], stat[:, 1, t:t + 1]))
                dve.scalar_tensor_tensor(out=finv[:, t, :], in0=finv[:, t, :], scalar=stat[:, 2, t:t + 1],
                                         in1=fgrow[:], op0=ALU.mult, op1=ALU.mult).then_inc(fin_ready, 1)


_INS = ['x', 'c', 'ctx', 'c_ctx', 'w_mod', 'b_mod', 'norm_mix_g', 'w_in', 'conv_q', 'conv_k', 'b_igate', 'b_fgate',
        'gmlp_ws', 'gmlp_bs', 'mlstm_norm_g', 'w_out', 'norm_ffn_g', 'w_router', 'w_gate_e', 'w_up_e', 'w_down_e',
        'final_g']


def kernel(**inputs):
    import numpy as np
    from concourse import bacc
    from concourse.bass_utils import run_bass_kernel_spmd

    nc = bacc.Bacc("TRN2", target_bir_lowering=False, num_devices=1)
    arrays, args = {}, []
    for name in _INS:
        a = np.ascontiguousarray(inputs[name])
        arrays[f"in_{name}"] = a
        args.append(nc.dram_tensor(f"in_{name}", a.shape, mybir.dt.from_np(a.dtype), kind="ExternalInput").ap())
    shape = inputs["x"].shape
    out = nc.dram_tensor("out_0", shape, F32, kind="ExternalOutput").ap()
    ffn_in = nc.dram_tensor("ffn_in", shape[1:], F32, kind="Internal").ap()
    stream = nc.dram_tensor("stream", shape[1:], F32, kind="Internal").ap()
    modrows = nc.dram_tensor("modrows", (1, 4 * shape[2]), F32, kind="Internal").ap()
    hybrid_block(nc, *args, out, ffn_in, stream, modrows)
    r = run_bass_kernel_spmd(nc, [arrays], core_ids=[0])
    return r.results[0]["out_0"]
```
